# Optimizing a Trainium2 kernel written in Bass

```python
import math
import jax, jax.numpy as jnp
from jax import lax
import numpy as np

D_MODEL = 1024
BATCH = 1
SEQ = 1024
DEPTH = 2

N_MIXERS = 2
N_A = (DEPTH + 1) // 2
N_B = DEPTH // 2
EPS = 1e-6
SC_WIDTH = 3
GDN_NK = 8
GDN_NV = 16
GDN_DK = 128
GDN_DV = 128
GDN_KEY_DIM = GDN_NK * GDN_DK
GDN_VALUE_DIM = GDN_NV * GDN_DV
GDN_QKV_DIM = 2 * GDN_KEY_DIM + GDN_VALUE_DIM
GDN_PROJ = GDN_QKV_DIM + GDN_VALUE_DIM + 2 * GDN_NV
GDN_CONV = 4
CHUNK = 64
D_FF = 2816
FFN_CONV = 3

kernel_name = 'hybrid_shortconv_gdn_convffn'

def rmsnorm(x, w):
    xf = x.astype(jnp.float32)
    y = xf * lax.rsqrt(jnp.mean(xf * xf, axis=-1, keepdims=True) + EPS)
    return (y * w.astype(jnp.float32)).astype(x.dtype)

def l2norm(x):
    return x * lax.rsqrt(jnp.sum(x * x, axis=-1, keepdims=True) + EPS)

def causal_dwconv(x, w):
    k_w, ch = w.shape
    return lax.conv_general_dilated(
        x, w.astype(x.dtype).reshape(k_w, 1, ch),
        window_strides=(1,), padding=[(k_w - 1, 0)],
        dimension_numbers=('NWC', 'WIO', 'NWC'),
        feature_group_count=ch)

def shortconv_mixer(h, w_in, conv_w, w_out):
    bcx = h @ w_in
    b_gate, c_gate, xv = jnp.split(bcx, 3, axis=-1)
    y = b_gate * causal_dwconv(c_gate * xv, conv_w)
    return y @ w_out

def gated_delta_rule_chunked(q, k, v, g, beta):
    bsz, s, h, dk = q.shape
    dv = v.shape[-1]
    n = s // CHUNK

    def chunks(t):
        return t.reshape(bsz, n, CHUNK, h, t.shape[-1]).transpose(1, 0, 3, 2, 4)

    qc, kc, vc = chunks(q), chunks(k), chunks(v)
    gc = jnp.cumsum(g.reshape(bsz, n, CHUNK, h).transpose(1, 0, 3, 2), axis=-1)
    bc = beta.reshape(bsz, n, CHUNK, h).transpose(1, 0, 3, 2)

    tril = jnp.tril(jnp.ones((CHUNK, CHUNK), dtype=bool))
    strict = jnp.tril(jnp.ones((CHUNK, CHUNK), dtype=bool), -1)
    diff = gc[..., :, None] - gc[..., None, :]
    decay = jnp.where(tril, jnp.exp(jnp.where(tril, diff, 0.0)), 0.0)

    kk = jnp.einsum('nbhid,nbhjd->nbhij', kc, kc)
    low = jnp.where(strict, bc[..., :, None] * kk * decay, 0.0)
    a_mat = jnp.eye(CHUNK, dtype=low.dtype) + low
    rhs = jnp.concatenate([vc * bc[..., None],
                           kc * (bc * jnp.exp(gc))[..., None]], axis=-1)
    sol = lax.linalg.triangular_solve(a_mat, rhs, left_side=True, lower=True,
                                      unit_diagonal=True)
    u, w = sol[..., :dv], sol[..., dv:]
    qk_intra = jnp.einsum('nbhid,nbhjd->nbhij', qc, kc) * decay
    q_dec = qc * jnp.exp(gc)[..., None]
    g_last = gc[..., -1]
    k_dec = kc * jnp.exp(g_last[..., None] - gc)[..., None]

    def step(state, xs):
        q_i, k_i, u_i, w_i, qk_i, gl_i = xs
        v_new = u_i - jnp.einsum('bhck,bhkv->bhcv', w_i, state)
        o_i = (jnp.einsum('bhck,bhkv->bhcv', q_i, state)
               + jnp.einsum('bhij,bhjv->bhiv', qk_i, v_new))
        state = (state * jnp.exp(gl_i)[..., None, None]
                 + jnp.einsum('bhck,bhcv->bhkv', k_i, v_new))
        return state, o_i

    state0 = jnp.zeros((bsz, h, dk, dv), dtype=q.dtype)
    _, o = lax.scan(step, state0, (q_dec, k_dec, u, w, qk_intra, g_last))
    return o.transpose(1, 0, 3, 2, 4).reshape(bsz, s, h, dv)

def gdn_mixer(h, w_in, conv_w, a_log, dt_bias, norm_w, w_out):
    bsz, s, _ = h.shape
    proj = h @ w_in
    qkv = proj[..., :GDN_QKV_DIM]
    z = proj[..., GDN_QKV_DIM:GDN_QKV_DIM + GDN_VALUE_DIM]
    a = proj[..., GDN_QKV_DIM + GDN_VALUE_DIM:GDN_QKV_DIM + GDN_VALUE_DIM + GDN_NV]
    b = proj[..., GDN_QKV_DIM + GDN_VALUE_DIM + GDN_NV:]
    qkv = jax.nn.silu(causal_dwconv(qkv, conv_w))
    q = qkv[..., :GDN_KEY_DIM].reshape(bsz, s, GDN_NK, GDN_DK).astype(jnp.float32)
    k = qkv[..., GDN_KEY_DIM:2 * GDN_KEY_DIM].reshape(bsz, s, GDN_NK, GDN_DK).astype(jnp.float32)
    v = qkv[..., 2 * GDN_KEY_DIM:].reshape(bsz, s, GDN_NV, GDN_DV).astype(jnp.float32)
    q = l2norm(q) * (GDN_DK ** -0.5)
    k = l2norm(k)
    rep = GDN_NV // GDN_NK
    q = jnp.repeat(q, rep, axis=2)
    k = jnp.repeat(k, rep, axis=2)
    beta = jax.nn.sigmoid(b.astype(jnp.float32))
    g = -jnp.exp(a_log.astype(jnp.float32)) * jax.nn.softplus(
        a.astype(jnp.float32) + dt_bias.astype(jnp.float32))
    o = gated_delta_rule_chunked(q, k, v, g, beta)
    o = rmsnorm(o, norm_w) * jax.nn.silu(z.reshape(bsz, s, GDN_NV, GDN_DV).astype(jnp.float32))
    return o.reshape(bsz, s, GDN_VALUE_DIM).astype(h.dtype) @ w_out

def conv_ffn(h, w_up, conv_w, w_down):
    u = causal_dwconv(h @ w_up, conv_w)
    gate, val = jnp.split(u, 2, axis=-1)
    return (jax.nn.silu(gate) * val) @ w_down

def setup_inputs(seed: int = 0) -> dict:
    key = jax.random.key(seed)
    ks = jax.random.split(key, 20)
    f32 = jnp.float32

    def nrm(k, shape, fan_in):
        return jax.random.normal(k, shape, f32) * (fan_in ** -0.5)

    def gain(k, shape):
        return 1.0 + 0.02 * jax.random.normal(k, shape, f32)

    x = jax.random.normal(ks[0], (BATCH, SEQ, D_MODEL), f32)
    norm_mix = gain(ks[1], (DEPTH, D_MODEL))
    norm_ffn = gain(ks[2], (DEPTH, D_MODEL))
    sc_w_in = nrm(ks[3], (N_A, D_MODEL, 3 * D_MODEL), D_MODEL)
    sc_conv = nrm(ks[4], (N_A, SC_WIDTH, D_MODEL), SC_WIDTH)
    sc_w_out = nrm(ks[5], (N_A, D_MODEL, D_MODEL), D_MODEL)
    gdn_w_in = nrm(ks[6], (N_B, D_MODEL, GDN_PROJ), D_MODEL)
    gdn_conv = nrm(ks[7], (N_B, GDN_CONV, GDN_QKV_DIM), GDN_CONV)
    gdn_a_log = jnp.log(jax.random.uniform(ks[8], (N_B, GDN_NV), f32, 1.0, 16.0))
    dt = jnp.exp(jax.random.uniform(ks[9], (N_B, GDN_NV), f32,
                                    math.log(0.001), math.log(0.1)))
    gdn_dt_bias = dt + jnp.log(-jnp.expm1(-dt))
    gdn_norm = gain(ks[10], (N_B, GDN_DV))
    gdn_w_out = nrm(ks[11], (N_B, GDN_VALUE_DIM, D_MODEL), GDN_VALUE_DIM)
    ffn_w_up = nrm(ks[12], (DEPTH, D_MODEL, 2 * D_FF), D_MODEL)
    ffn_conv = nrm(ks[13], (DEPTH, FFN_CONV, 2 * D_FF), FFN_CONV)
    ffn_w_down = nrm(ks[14], (DEPTH, D_FF, D_MODEL), D_FF)
    norm_final = gain(ks[15], (D_MODEL,))
    return {'x': x, 'norm_mix': norm_mix, 'norm_ffn': norm_ffn,
            'sc_w_in': sc_w_in, 'sc_conv': sc_conv, 'sc_w_out': sc_w_out,
            'gdn_w_in': gdn_w_in, 'gdn_conv': gdn_conv, 'gdn_a_log': gdn_a_log,
            'gdn_dt_bias': gdn_dt_bias, 'gdn_norm': gdn_norm, 'gdn_w_out': gdn_w_out,
            'ffn_w_up': ffn_w_up, 'ffn_conv': ffn_conv, 'ffn_w_down': ffn_w_down,
            'norm_final': norm_final}

def reference(x, norm_mix, norm_ffn, sc_w_in, sc_conv, sc_w_out,
              gdn_w_in, gdn_conv, gdn_a_log, gdn_dt_bias, gdn_norm, gdn_w_out,
              ffn_w_up, ffn_conv, ffn_w_down, norm_final):
    for i in range(DEPTH):
        h = rmsnorm(x, norm_mix[i])
        j = i // N_MIXERS
        if i % N_MIXERS == 0:
            mix = shortconv_mixer(h, sc_w_in[j], sc_conv[j], sc_w_out[j])
        else:
            mix = gdn_mixer(h, gdn_w_in[j], gdn_conv[j], gdn_a_log[j], gdn_dt_bias[j],
                            gdn_norm[j], gdn_w_out[j])
        x = x + mix
        h = rmsnorm(x, norm_ffn[i])
        x = x + conv_ffn(h, ffn_w_up[i], ffn_conv[i], ffn_w_down[i])
    return rmsnorm(x, norm_final)


_drawn_inputs = setup_inputs


def setup_inputs(seed=0):
    import zlib

    import numpy as np

    out = dict(_drawn_inputs(seed))
    spreads = {}
    factors = {'norm_ffn': 3.232, 'gdn_norm': 29.78, 'norm_final': 8.195}
    for name, (base, spread) in spreads.items():
        noise = np.random.default_rng([zlib.crc32(name.encode()), seed]).standard_normal(out[name].shape)
        drawn = base * np.exp(spread * noise) if base else spread * noise
        out[name] = __import__('jax').numpy.asarray(drawn.astype(out[name].dtype))
    for name, factor in factors.items():
        out[name] = (out[name] * factor).astype(out[name].dtype)
    return out
```

```python
import concourse.bass as bass
from concourse import mybir
from contextlib import ExitStack

F32 = mybir.dt.float32
F32R = mybir.dt.float32r
ALU = mybir.AluOpType
ACT = mybir.ActivationFunctionType
AX = mybir.AxisListType

P = 128
SEQ = 1024
D = 1024
KT = D // P
HALF = 512
NHALF = SEQ // HALF
EPS = 1e-6
SC_TAPS = 3
NK, NV, DK, DV = 8, 16, 128, 128
GDN_TAPS = 4
QKV = 2 * NK * DK + NV * DV
QKV_T = QKV // P
GPROJ = QKV + NV * DV + 2 * NV
D_FF = 2816
FT = D_FF // P
FFN_TAPS = 3
C = 128
NC = SEQ // C
BIG = 1e30
WCOLS = 1024


def wait(engine, semaphore, value):
    if not isinstance(value, int) or value > 0:
        engine.wait_ge(semaphore, value)


def wait_before_address(sp, semaphore, value):
    if not isinstance(value, int) or value > 0:
        sp.wait_ge(semaphore, value)
        sp.nop(nofuse=True)


def build_weight_stream(sems, mem, tag):
    w_in = [sems(f"{tag}_w_in{s}") for s in range(2)]
    w_hi = sems(f"{tag}_w_hi")
    w_lo = sems(f"{tag}_w_lo")

    def load(sp, m, s, src):
        wait_before_address(sp, w_lo, 2 * m + s - 1)
        width = src.shape[1] * src.shape[2]
        sp.dma_start(mem.raw[:, s, 0:width].rearrange("p (k n) -> p k n", k=src.shape[1]),
                     src).then_inc(w_in[s], 16)

    def split_hi(act, m, s, done, value):
        act.wait_ge(w_in[s], 16 * m + 16)
        wait(act, done, value)
        act.activation(mem.wh[s][:, :], mem.raw[:, s, :], ACT.Copy).then_inc(w_hi, 1)

    def split_lo(pool, m, s):
        pool.wait_ge(w_hi, 2 * m + s + 1)
        pool.tensor_tensor(mem.wl[s][:, :], mem.raw[:, s, :], mem.wh[s][:, :].bitcast(F32),
                           ALU.subtract).then_inc(w_lo, 1)

    def ready(pe, m, s):
        pe.wait_ge(w_lo, 2 * m + s + 1)

    return load, split_hi, split_lo, ready, w_in


def products(pe, out, pairs):
    last = None
    for k, (wh, wl, ah, al) in enumerate(pairs):
        pe.matmul(out, wh, ah, start=(k == 0), stop=False)
        pe.matmul(out, wh, al, start=False, stop=False)
        last = pe.matmul(out, wl, ah, start=False, stop=(k == len(pairs) - 1))
    return last


def in_tile(pe, mem, s, hf, bank):
    cols = slice(hf * HALF, (hf + 1) * HALF)
    return products(pe, mem.ps[:, bank, :],
                    [(mem.wh[s][:, k * P:(k + 1) * P], mem.wl[s][:, k * P:(k + 1) * P],
                      mem.xh[:, k, cols], mem.xl[:, k, cols]) for k in range(KT)])


def out_tile(pe, mem, s, m, hf, bank):
    cols = slice(hf * HALF, (hf + 1) * HALF)
    return products(pe, mem.ps[:, bank, :],
                    [(mem.wh[s][:, k * 512 + m * P:k * 512 + (m + 1) * P],
                      mem.wl[s][:, k * 512 + m * P:k * 512 + (m + 1) * P],
                      mem.ah[:, k, cols], mem.al[:, k, cols]) for k in range(2)])


def build_norm(nc, sems, mem, gain, tag):
    hi = sems(f"{tag}_x_hi")
    sq = sems(f"{tag}_x_sq")
    lo = sems(f"{tag}_x_lo")
    summed = sems(f"{tag}_x_sum")
    root = sems(f"{tag}_x_root")
    rms = sems(f"{tag}_x_rms")

    def scalar(act):
        for m in range(KT):
            act.activation(mem.xh[:, m, :], mem.x[:, m, :], ACT.Copy,
                           scale=mem.par[:, gain + m:gain + m + 1]).then_inc(hi, 1)
            if m >= 2:
                act.wait_ge(summed, m - 1)
            act.activation(mem.sq[:, m % 2, :], mem.x[:, m, :], ACT.Square).then_inc(sq, 1)
        act.wait_ge(summed, KT)
        for hf in range(NHALF):
            act.activation(mem.R[:, hf * HALF:(hf + 1) * HALF], mem.ps[:, 4 + hf, :], ACT.Sqrt,
                           scale=1.0 / D, bias=mem.eps[:, 0:1]).then_inc(root, 1)

    def vector(dve):
        for m in range(KT):
            dve.wait_ge(hi, m + 1)
            dve.scalar_tensor_tensor(out=mem.xl[:, m, :], in0=mem.x[:, m, :],
                                     scalar=mem.par[:, gain + m:gain + m + 1],
                                     in1=mem.xh[:, m, :].bitcast(F32),
                                     op0=ALU.mult, op1=ALU.subtract).then_inc(lo, 1)
        for hf in range(NHALF):
            dve.wait_ge(root, hf + 1)
            dve.reciprocal(mem.R[:, hf * HALF:(hf + 1) * HALF],
                           mem.R[:, hf * HALF:(hf + 1) * HALF]).then_inc(rms, 1)

    def tensor(pe):
        for m in range(KT):
            pe.wait_ge(sq, m + 1)
            for hf in range(NHALF):
                last = pe.matmul(mem.ps[:, 4 + hf, :], mem.ones[:, :],
                                 mem.sq[:, m % 2, hf * HALF:(hf + 1) * HALF],
                                 start=(m == 0), stop=(m == KT - 1))
            last.then_inc(summed, 1)
        pe.wait_ge(lo, KT)

    return scalar, vector, tensor, root, rms


def phase_load(nc, sems, mem, io):
    with ExitStack() as ctx:
        stage = ctx.enter_context(nc.sbuf_tensor("stage", [P, NC, D], F32))
        pstage = ctx.enter_context(nc.sbuf_tensor("pstage", [P, 5, P], F32))
        x_in = sems("load_x_in")
        p_in = sems("load_p_in")
        made = sems("load_const")
        turned = sems("load_turned")
        kept_v = sems("load_kept_v")
        kept_a = sems("load_kept_a")
        block = ctx.enter_context(nc.Block())
        rows = mem.par_rows
        ffn_rows = rows["ffn"] // 3

        @block.sync
        def _(sp):
            for c in range(NC):
                sp.dma_start(stage[:, c, :], io.x[0, c * P:(c + 1) * P, :]).then_inc(x_in, 16)
            sp.wait_ge(x_in, 16 * NC)

        @block.scalar
        def _(act):
            act.dma_start(pstage[0:16, 0, :], io.norm_mix.rearrange("l (m p) -> (l m) p", p=P)).then_inc(p_in, 16)
            act.dma_start(pstage[16:32, 0, :], io.norm_ffn.rearrange("l (m p) -> (l m) p", p=P)).then_inc(p_in, 16)
            act.dma_start(pstage[32:40, 0, :], io.norm_final.rearrange("(m p) -> m p", p=P)).then_inc(p_in, 16)
            act.dma_start(pstage[40:64, 0, :], io.sc_conv.rearrange("l t (m p) -> (l t m) p", p=P)).then_inc(p_in, 16)
            act.dma_start(pstage[64:65, 0, :], io.gdn_norm).then_inc(p_in, 16)
            act.dma_start(pstage[:, 1, :], io.gdn_conv.rearrange("l t (m p) -> (l t m) p", p=P)).then_inc(p_in, 16)
            fc = io.ffn_conv.rearrange("l t (m p) -> (l t m) p", p=P)
            for g in range(3):
                act.dma_start(pstage[0:ffn_rows, 2 + g, :],
                              fc[g * ffn_rows:(g + 1) * ffn_rows, :]).then_inc(p_in, 16)
            act.dma_start(mem.alog[:, :], io.gdn_a_log.partition_broadcast(P)).then_inc(p_in, 16)
            act.dma_start(mem.dtb[:, :], io.gdn_dt_bias.partition_broadcast(P)).then_inc(p_in, 16)
            act.wait_ge(p_in, 16 * 11)
            for t in range(1, 2 * KT, 2):
                act.wait_ge(turned, 3 + t)
                act.activation(mem.x[:, t // 2, (t % 2) * HALF:(t % 2 + 1) * HALF], mem.ps[:, t % 8, :],
                               ACT.Copy).then_inc(kept_a, 1)

        @block.gpsimd
        def _(pool):
            pool.memset(mem.ones[:, :], 1.0).then_inc(made, 1)
            pool.memset(mem.ident[:, :], 0.0).then_inc(made, 1)
            pool.memset(mem.eps[:, :], EPS).then_inc(made, 1)
            pool.wait_ge(made, 2)
            pool.affine_select(out=mem.ident[:, :], in_=mem.ident[:, :], compare_op=ALU.not_equal, fill=1.0,
                               base=0, pattern=[[-1, P]], channel_multiplier=1).then_inc(made, 1)

        @block.vector
        def _(dve):
            dve.wait_ge(turned, 1)
            dve.tensor_copy(mem.par[:, :], mem.ps[:, 0, 0:rows["par"]]).then_inc(kept_v, 1)
            dve.tensor_copy(mem.gcw[:, :], mem.ps[:, 0, P:2 * P]).then_inc(kept_v, 1)
            dve.wait_ge(turned, 2)
            dve.tensor_copy(mem.fcw[:, :], mem.ps[:, 1, 0:rows["ffn"]]).then_inc(kept_v, 1)
            for t in range(0, 2 * KT, 2):
                dve.wait_ge(turned, 3 + t)
                dve.tensor_copy(mem.x[:, t // 2, (t % 2) * HALF:(t % 2 + 1) * HALF],
                                mem.ps[:, t % 8, :]).then_inc(kept_v, 1)

        @block.tensor
        def _(pe):
            pe.wait_ge(made, 4)
            pe.wait_ge(p_in, 16 * 11)
            pe.transpose(mem.ps[:, 0, 0:rows["par"]], pstage[0:rows["par"], 0, :],
                         mem.ident[0:rows["par"], 0:rows["par"]])
            pe.transpose(mem.ps[:, 0, P:2 * P], pstage[:, 1, :], mem.ident[:, :]).then_inc(turned, 1)
            for g in range(3):
                last = pe.transpose(mem.ps[:, 1, g * ffn_rows:(g + 1) * ffn_rows], pstage[0:ffn_rows, 2 + g, :],
                                    mem.ident[0:ffn_rows, 0:ffn_rows])
            last.then_inc(turned, 1)
            pe.wait_ge(x_in, 16 * NC)
            for t in range(2 * KT):
                if t in (0, 1):
                    pe.wait_ge(kept_v, 2 + t)
                elif t >= 8 and t % 2 == 0:
                    pe.wait_ge(kept_v, 3 + (t - 8) // 2 + 1)
                elif t >= 8:
                    pe.wait_ge(kept_a, (t - 8) // 2 + 1)
                for q in range(4):
                    c = (t % 2) * 4 + q
                    last = pe.transpose(mem.ps[:, t % 8, q * P:(q + 1) * P],
                                        stage[:, c, (t // 2) * P:(t // 2 + 1) * P], mem.ident[:, :])
                last.then_inc(turned, 1)


def convolve(dve, dst, src, taps, tap, base):
    last = len(taps) - 1
    dve.tensor_scalar(dst, src[:, last:last + SEQ], taps[last], None, ALU.mult).then_inc(tap, 1)
    for n, k in enumerate(reversed(range(last))):
        dve.wait_ge(tap, base + n + 1)
        dve.scalar_tensor_tensor(out=dst, in0=src[:, k:k + SEQ], scalar=taps[k], in1=dst,
                                 op0=ALU.mult, op1=ALU.add).then_inc(tap, 1)


def phase_mix(nc, sems, mem, io, kind, layer):
    ffn = kind == "ffn"
    tag = f"{kind}{layer}"
    R = 2 if ffn else 3
    U = 2 * R
    STEPS = (FT if ffn else KT) // 2
    TILES = 2 * U + 16
    PAD = 2
    w_up = (io.ffn_w_up[layer] if ffn else io.sc_w_in[0]).rearrange("(k p) n -> p k n", p=P)
    w_down = io.ffn_w_down[layer] if ffn else io.sc_w_out[0]
    with ExitStack() as ctx:
        def sb(name, shape, dt=F32):
            return ctx.enter_context(nc.sbuf_tensor(f"{tag}_{name}", shape, dt))

        mem.xh, mem.xl = sb("xh", [P, KT, SEQ], F32R), sb("xl", [P, KT, SEQ], F32R)
        mem.ah, mem.al = sb("ah", [P, 2, SEQ], F32R), sb("al", [P, 2, SEQ], F32R)
        mem.sq, mem.R = sb("sq", [P, 2, SEQ]), sb("R", [P, SEQ])
        padded = [sb(f"pad{b}", [P, PAD + SEQ]) for b in range(2)]
        conved = sb("conved", [P, SEQ])
        hidden = sb("hidden", [P, SEQ])
        scratch = None if ffn else sb("scratch", [P, SEQ])
        cgate = None if ffn else sb("cgate", [P, SEQ])

        load, split_hi, split_lo, ready, _ = build_weight_stream(sems, mem, tag)
        norm_scalar, norm_vector, norm_tensor, root, rms = build_norm(
            nc, sems, mem, (16 if ffn else 0) + 8 * layer, tag)
        zeroed = sems(f"{tag}_zeroed")
        tile = sems(f"{tag}_tile")
        kept = sems(f"{tag}_kept")
        product = sems(f"{tag}_product")
        tap = sems(f"{tag}_tap")
        silu = sems(f"{tag}_silu")
        gated = sems(f"{tag}_gated")
        a_hi = sems(f"{tag}_a_hi")
        a_lo = sems(f"{tag}_a_lo")
        added = sems(f"{tag}_added")
        block = ctx.enter_context(nc.Block())

        def ups(last):
            return U - 1 if last else U

        def use(i, q):
            return ((U + 2) // 2) * i + (1 + q) // 2, (1 + q) % 2

        def tiles_before(i, q, last):
            return TILES * i + 2 + 2 * min(q, ups(last)) + 8 * max(0, q - ups(last))

        def up_src(i, k):
            f, r = (1 + k) // R, (1 + k) % R
            part = (0, D_FF)[r] if ffn else (D, 2 * D, 0)[r]
            return w_up[:, :, bass.ds(2 * P * i + (f * P + part), P)]

        def down_src(i, o):
            return w_down[bass.ds(2 * P * i, 2 * P), o * HALF:(o + 1) * HALF].rearrange("(k p) n -> p k n", p=P)

        def steps(engine, step):
            step(0, False)
            with engine.Fori(1, STEPS - 1) as i:
                step(i, False)
            step(STEPS - 1, True)

        @block.sync
        def _(sp):
            def step(i, last):
                for q in range(ups(last) + 2):
                    src = up_src(i, q) if q < ups(last) else down_src(i, q - ups(last))
                    load(sp, *use(i, q), src)

            load(sp, 0, 0, up_src(0, -1))
            steps(sp, step)

        @block.gpsimd
        def _(pool):
            for b in range(2):
                pool.memset(padded[b][:, 0:PAD], 0.0).then_inc(zeroed, 1)

            def step(i, last):
                for q in range(ups(last) + 2):
                    if q < ups(last) + 1:
                        split_lo(pool, *use(i, q + 1))
                    elif not last:
                        split_lo(pool, *use(i, q + 1))
                    if q < U and q % R == R - 1:
                        f = q // R
                        pool.wait_ge(a_hi, 2 * i + f + 1)
                        pool.tensor_tensor(mem.al[:, f, :], hidden[:, :], mem.ah[:, f, :].bitcast(F32),
                                           ALU.subtract).then_inc(a_lo, 1)

            split_lo(pool, 0, 0)
            split_lo(pool, 0, 1)
            steps(pool, step)

        @block.scalar
        def _(act):
            def step(i, last):
                for q in range(ups(last) + 2):
                    if q < ups(last) + 1 or not last:
                        split_hi(act, *use(i, q + 1), tile, tiles_before(i, q, last))
                    f = q // R
                    if ffn and q < U and q % R == 0:
                        act.wait_ge(tap, 6 * (2 * i + f) + 3)
                        act.activation(conved[:, :], conved[:, :], ACT.Silu).then_inc(silu, 1)
                    if q < U and q % R == R - 1:
                        act.wait_ge(gated, 2 * i + f + 1)
                        wait(act, tile, TILES * i + 2 if f == 0 and not (isinstance(i, int) and i == 0) else 0)
                        act.activation(mem.ah[:, f, :], hidden[:, :], ACT.Copy).then_inc(a_hi, 1)

            split_hi(act, 0, 0, tile, 0)
            split_hi(act, 0, 1, tile, 0)
            norm_scalar(act)
            steps(act, step)

        @block.vector
        def _(dve):
            def keep(i, k, hf, dst):
                cols = slice(hf * HALF, (hf + 1) * HALF)
                t = 2 * (1 + k) + hf
                dve.wait_ge(tile, TILES * i + t + 1)
                dve.tensor_tensor(dst, mem.ps[:, t % 4, :], mem.R[:, cols], ALU.mult).then_inc(kept, 1)

            def kept_both(i, k):
                dve.wait_ge(kept, 2 * U * i + 2 * (1 + k) + 2)

            def ffn_job(i, k):
                r, f = (1 + k) % R, (1 + k) // R
                u = U * i + (1 + k)
                wait(dve, tap, 3 * u - 3)
                for hf in range(NHALF):
                    keep(i, k, hf, padded[r][:, PAD + hf * HALF:PAD + (hf + 1) * HALF])
                kept_both(i, k)
                taps = [mem.fcw[:, bass.ds((layer * FFN_TAPS + j) * 2 * FT + r * FT + 2 * i + f, 1)]
                        for j in range(FFN_TAPS)]
                if r == 0:
                    wait(dve, gated, 2 * i + f)
                    convolve(dve, conved[:, :], padded[0], taps, tap, 3 * u)
                else:
                    wait(dve, a_lo, 2 * i + f)
                    convolve(dve, hidden[:, :], padded[1], taps, tap, 3 * u)
                    dve.wait_ge(tap, 3 * u + 3)
                    dve.wait_ge(silu, 2 * i + f + 1)
                    dve.tensor_tensor(hidden[:, :], hidden[:, :], conved[:, :], ALU.mult).then_inc(gated, 1)

            def sc_job(i, k):
                r, f = (1 + k) % R, (1 + k) // R
                if r == 0:
                    wait(dve, product, 2 * i + f)
                    for hf in range(NHALF):
                        keep(i, k, hf, cgate[:, hf * HALF:(hf + 1) * HALF])
                elif r == 1:
                    wait(dve, gated, 2 * i + f)
                    for hf in range(NHALF):
                        keep(i, k, hf, scratch[:, hf * HALF:(hf + 1) * HALF])
                    kept_both(i, k)
                    wait(dve, tap, 3 * (2 * i + f))
                    dve.tensor_tensor(padded[0][:, PAD:PAD + SEQ], scratch[:, :], cgate[:, :],
                                      ALU.mult).then_inc(product, 1)
                    dve.wait_ge(product, 2 * i + f + 1)
                    convolve(dve, conved[:, :], padded[0],
                             [mem.par[:, bass.ds(40 + 8 * j + 2 * i + f, 1)] for j in range(SC_TAPS)],
                             tap, 3 * (2 * i + f))
                else:
                    dve.wait_ge(product, 2 * i + f + 1)
                    for hf in range(NHALF):
                        keep(i, k, hf, scratch[:, hf * HALF:(hf + 1) * HALF])
                    kept_both(i, k)
                    dve.wait_ge(tap, 3 * (2 * i + f) + 3)
                    wait(dve, a_lo, 2 * i + f)
                    dve.tensor_tensor(hidden[:, :], conved[:, :], scratch[:, :], ALU.mult).then_inc(gated, 1)

            def step(i, last):
                for k in range(ups(last)):
                    (ffn_job if ffn else sc_job)(i, k)
                for t in range(2 * KT):
                    dve.wait_ge(tile, tiles_before(i, ups(last), last) + t + 1)
                    cols = slice((t % 2) * HALF, (t % 2 + 1) * HALF)
                    dve.tensor_tensor(mem.x[:, t // 2, cols], mem.ps[:, 4 + t % 4, :], mem.x[:, t // 2, cols],
                                      ALU.add).then_inc(added, 1)

            norm_vector(dve)
            dve.wait_ge(rms, NHALF)
            dve.wait_ge(zeroed, 2)
            (ffn_job if ffn else sc_job)(0, -1)
            steps(dve, step)

        @block.tensor
        def _(pe):
            def up_job(i, k, m, s):
                ready(pe, m, s)
                for hf in range(NHALF):
                    t = 2 * (1 + k) + hf
                    wait(pe, kept, 2 * U * i + t - 3)
                    in_tile(pe, mem, s, hf, t % 4).then_inc(tile, 1)

            def step(i, last):
                for k in range(ups(last)):
                    up_job(i, k, *use(i, k))
                pe.wait_ge(a_lo, 2 * i + 2)
                for o in range(2):
                    m, s = use(i, ups(last) + o)
                    ready(pe, m, s)
                    for t in range(8 * o, 8 * o + 8):
                        wait(pe, added, 16 * i + t - 3)
                        out_tile(pe, mem, s, (t // 2) % 4, t % 2, 4 + t % 4).then_inc(tile, 1)

            norm_tensor(pe)
            up_job(0, -1, 0, 0)
            pe.wait_ge(root, NHALF)
            steps(pe, step)


def phase_gdn(nc, sems, mem, io):
    with ExitStack() as ctx:
        def sb(name, shape, dt=F32):
            return ctx.enter_context(nc.sbuf_tensor(f"gdn_{name}", shape, dt))

        mem.gates = sb("gates", [P, len(GATES), NV * NC])
        mem.ab = sb("ab", [P, SEQ])
        mem.upper = sb("upper", [P, P])
        mem.neg = sb("neg", [P, P])
        mem.mask = [sb(f"mask{l}", [P, P]) for l in range(LEVELS)]
        mem.dram = {name: nc.dram_tensor(f"scratch_{name}", shape, F32).ap()
                    for name, shape in (("qT", [NK, P, SEQ]), ("kT", [NK, P, SEQ]), ("k", [NK, P, SEQ]),
                                        ("v", [NV, P, SEQ]), ("z", [NV, P, SEQ]))}
        gdn_project(nc, sems, mem, io)
        gdn_gates(nc, sems, mem)
        gdn_mix(nc, sems, mem, io)


GATES = ("g", "beta", "neg_gc", "eg", "neg_eg", "beta_ekd", "egl")
LEVELS = 7


def make_masks(pool, mem, made):
    n = 0
    for m, value in [(mem.upper, 1.0), (mem.neg, 0.0)] + [(m, 1.0) for m in mem.mask]:
        pool.memset(m[:, :], value).then_inc(made, 1)
        n += 1
    pool.wait_ge(made, n)
    pool.affine_select(out=mem.upper[:, :], in_=mem.upper[:, :], compare_op=ALU.is_ge, fill=0.0, base=0,
                       pattern=[[1, P]], channel_multiplier=-1).then_inc(made, 1)
    pool.affine_select(out=mem.neg[:, :], in_=mem.neg[:, :], compare_op=ALU.is_ge, fill=-BIG, base=0,
                       pattern=[[1, P]], channel_multiplier=-1).then_inc(made, 1)
    n += 2
    for l in range(LEVELS):
        s = 1 << l
        view = mem.mask[l][:, :].rearrange("p (b r) -> p b r", r=2 * s)
        blocks = P // (2 * s)
        for base, channel, pattern in ((0, 1, [[-2 * s, blocks], [0, 2 * s]]),
                                       (s - 1, -1, [[2 * s, blocks], [0, 2 * s]]),
                                       (-s, 0, [[0, blocks], [1, 2 * s]])):
            pool.affine_select(out=view, in_=view, compare_op=ALU.is_ge, fill=0.0, base=base,
                               pattern=pattern, channel_multiplier=channel).then_inc(made, 1)
            n += 1
            pool.wait_ge(made, n)


def gdn_project(nc, sems, mem, io):
    tag = "gp"
    PAD = GDN_TAPS - 1
    w_in = io.gdn_w_in[0].rearrange("(k p) n -> p k n", p=P)
    with ExitStack() as ctx:
        def sb(name, shape, dt=F32):
            return ctx.enter_context(nc.sbuf_tensor(f"{tag}_{name}", shape, dt))

        mem.R = sb("R", [P, SEQ])
        mem.xh, mem.xl = sb("xh", [P, KT, SEQ], F32R), sb("xl", [P, KT, SEQ], F32R)
        padded = [sb(f"pad{b}", [P, PAD + SEQ]) for b in range(2)]
        act_in = [sb(f"conved{b}", [P, SEQ]) for b in range(2)]
        mem.sq = sb("sq", [P, 2, SEQ])
        tok = [sb(f"tok{e}", [P, SEQ]) for e in range(4)]
        back = [sb(f"back{e}", [P, SEQ]) for e in range(2)]
        zbuf = [sb(f"z{e}", [P, SEQ]) for e in range(2)]
        inv = [sb(f"inv{e}", [P, NC]) for e in range(2)]
        qeps = sb("qeps", [P, 2])

        load, split_hi, split_lo, ready, w_in_landed = build_weight_stream(sems, mem, tag)
        norm_scalar, norm_vector, norm_tensor, root, rms = build_norm(nc, sems, mem, 8, tag)
        made = sems(f"{tag}_made")
        zeroed = sems(f"{tag}_zeroed")
        tile = sems(f"{tag}_tile")
        kept = sems(f"{tag}_kept")
        tap = sems(f"{tag}_tap")
        silu = sems(f"{tag}_silu")
        turned = sems(f"{tag}_turned")
        held = sems(f"{tag}_held")
        square = sems(f"{tag}_square")
        norm2 = sems(f"{tag}_norm2")
        norm = sems(f"{tag}_norm")
        inverse = sems(f"{tag}_inverse")
        normed = sems(f"{tag}_normed")
        stored = {b: sems(f"{tag}_stored_{b}") for b in ("back0", "back1", "tok1", "tok2", "tok3", "z0", "z1")}
        block = ctx.enter_context(nc.Block())

        TURNS = ((1, "tok", 0), (2, "tok", 1), (3, "tok", 2), (4, "tok", 3), (4, "back", 0), (5, "back", 1))

        def use(h, k):
            return 3 * h + (1 + k) // 2, (1 + k) % 2

        def src(h, k):
            base = (0, NK * DK, 2 * NK * DK, 2 * NK * DK + DV, QKV, QKV + DV)[k]
            return w_in[:, :, bass.ds(h * (P if k < 2 else 2 * P) + base, P)]

        def steps(engine, step):
            step(0)
            with engine.Fori(1, NK) as h:
                step(h)

        @block.sync
        def _(sp):
            def store(h, k):
                def put(name, buffer, index, key):
                    sp.dma_start(mem.dram[name][bass.ds(index, 1), :, :].rearrange("o p n -> (o p) n"),
                                 buffer[:, :]).then_inc(stored[key], 16)
                if k == 0:
                    wait_before_address(sp, held, 12 * h + 10)
                    put("qT", back[0], h, "back0")
                elif k == 1:
                    wait_before_address(sp, normed, 2 * h + 2)
                    put("k", tok[1], h, "tok1")
                    wait_before_address(sp, held, 12 * h + 12)
                    put("kT", back[1], h, "back1")
                elif k in (2, 3):
                    wait_before_address(sp, held, 12 * h + (6 if k == 2 else 8))
                    put("v", tok[k], 2 * h + k - 2, f"tok{k}")
                else:
                    wait_before_address(sp, silu, 6 * h + k + 1)
                    put("z", zbuf[k - 4], 2 * h + k - 4, f"z{k - 4}")

            sp.wait_ge(zeroed, 5)
            sp.dma_start(mem.raw[:, 0, :].rearrange("p (k n) -> p k n", k=KT)[:, :, 0:2 * NV],
                         w_in[:, :, QKV + NV * DV:GPROJ]).then_inc(w_in_landed[0], 16)
            for k in range(6):
                load(sp, *use(0, k), src(0, k))
            with sp.Fori(1, NK) as h:
                for k in range(6):
                    load(sp, *use(h, k), src(h, k))
                    store(h - 1, k)
            for k in range(6):
                store(NK - 1, k)
            for key in stored:
                sp.wait_ge(stored[key], 16 * NK)

        @block.gpsimd
        def _(pool):
            for b in range(2):
                pool.memset(padded[b][:, 0:PAD], 0.0).then_inc(zeroed, 1)
            pool.memset(mem.raw[:, 0, :], 0.0).then_inc(zeroed, 1)
            pool.memset(qeps[:, 0:1], EPS * DK).then_inc(zeroed, 1)
            pool.memset(qeps[:, 1:2], EPS).then_inc(zeroed, 1)
            split_lo(pool, 0, 0)
            split_lo(pool, 0, 1)
            make_masks(pool, mem, made)

            for k in range(6):
                split_lo(pool, *use(0, k + 1))
            with pool.Fori(1, NK - 1) as h:
                for k in range(6):
                    split_lo(pool, *use(h, k + 1))
            for k in range(5):
                split_lo(pool, *use(NK - 1, k + 1))

        @block.scalar
        def _(act):
            def hold(h, e, b):
                _, what, n = TURNS[e]
                act.wait_ge(turned, 12 * h + 2 * e + b + 1)
                if b == 0 and not (isinstance(h, int) and h == 0):
                    key = f"{what}{n}"
                    if key in stored:
                        act.wait_ge(stored[key], 16 * h)
                dst = (tok if what == "tok" else back)[n]
                act.activation(dst[:, b * HALF:(b + 1) * HALF], mem.ps[:, 4 + 2 * (e % 2) + b, :],
                               ACT.Copy).then_inc(held, 1)

            def root_of(h, e):
                act.wait_ge(norm2, 2 * h + e + 1)
                act.activation(inv[e][:, :], inv[e][:, :], ACT.Sqrt, scale=float(DK) if e == 0 else 1.0,
                               bias=qeps[:, e:e + 1]).then_inc(norm, 1)

            def step(h, last):
                for k in range(6):
                    if k < 5 or not last:
                        split_hi(act, *use(h, k + 1), tile, 2 * (6 * h + k) + 2)
                    if k >= 1:
                        do_silu(h, k - 1)
                    if k == 4:
                        root_of(h, 0)
                        root_of(h, 1)
                    for e, (after, what, n) in enumerate(TURNS):
                        if after == k:
                            hold(h, e, 0)
                            hold(h, e, 1)
                do_silu(h, 5)

            def do_silu(h, k):
                if k < 4:
                    act.wait_ge(tap, 16 * h + 4 * k + 4)
                    act.activation(act_in[k % 2][:, :], act_in[k % 2][:, :], ACT.Silu).then_inc(silu, 1)
                else:
                    act.wait_ge(kept, 12 * h + 2 * k + 4)
                    act.activation(zbuf[k - 4][:, :], zbuf[k - 4][:, :], ACT.Silu).then_inc(silu, 1)

            split_hi(act, 0, 0, tile, 0)
            split_hi(act, 0, 1, tile, 0)
            norm_scalar(act)
            act.wait_ge(zeroed, 5)
            step(0, False)
            with act.Fori(1, NK - 1) as h:
                step(h, False)
            step(NK - 1, True)

        @block.vector
        def _(dve):
            def keep(h, k, hf, dst):
                t = 12 * h + 2 * (1 + k) + hf
                cols = slice(hf * HALF, (hf + 1) * HALF)
                dve.wait_ge(tile, t + 1)
                dve.tensor_tensor(dst, mem.ps[:, (2 * (1 + k) + hf) % 4, :], mem.R[:, cols],
                                  ALU.mult).then_inc(kept, 1)

            def conv_job(h, k):
                b = k % 2
                wait(dve, tap, 16 * h + 4 * (k - 1))
                for hf in range(NHALF):
                    keep(h, k, hf, padded[b][:, PAD + hf * HALF:PAD + (hf + 1) * HALF])
                dve.wait_ge(kept, 12 * h + 2 * (1 + k) + 2)
                if k >= 2:
                    dve.wait_ge(turned, 12 * h + 2 * (k - 2) + 2)
                elif not (isinstance(h, int) and h == 0):
                    dve.wait_ge(turned, 12 * (h - 1) + (6 if k == 0 else 8))
                first = QT[k]
                taps = [mem.gcw[:, bass.ds(j * QKV_T + first + h * (1 if k < 2 else 2), 1)]
                        for j in range(GDN_TAPS)]
                convolve(dve, act_in[b][:, :], padded[b], taps, tap, 16 * h + 4 * k)

            QT = (0, NK, 2 * NK, 2 * NK + 1)

            def sums(h, e):
                dve.wait_ge(held, 12 * h + 2 * e + 2)
                wait(dve, norm2, 2 * h + e - 1)
                dve.tensor_tensor(mem.sq[:, e, :], tok[e][:, :], tok[e][:, :], ALU.mult).then_inc(square, 1)
                dve.wait_ge(square, 2 * h + e + 1)
                wait(dve, normed, 2 * h + e - 1)
                dve.tensor_reduce(inv[e][:, :], mem.sq[:, e, :].rearrange("p (c d) -> p c d", c=NC), AX.X,
                                  ALU.add).then_inc(norm2, 1)

            def scale(h, e):
                dve.wait_ge(norm, 2 * h + e + 1)
                dve.reciprocal(inv[e][:, :], inv[e][:, :]).then_inc(inverse, 1)
                dve.wait_ge(inverse, 2 * h + e + 1)
                view = tok[e][:, :].rearrange("p (c d) -> p c d", c=NC)
                dve.tensor_tensor(view, view, inv[e][:, :].unsqueeze(2).to_broadcast([P, NC, DK]),
                                  ALU.mult).then_inc(normed, 1)

            def z_job(h, k):
                if not (isinstance(h, int) and h == 0):
                    dve.wait_ge(stored[f"z{k - 4}"], 16 * h)
                for hf in range(NHALF):
                    keep(h, k, hf, zbuf[k - 4][:, hf * HALF:(hf + 1) * HALF])

            def step(h):
                conv_job(h, 0)
                conv_job(h, 1)
                sums(h, 0)
                conv_job(h, 2)
                sums(h, 1)
                conv_job(h, 3)
                scale(h, 0)
                scale(h, 1)
                z_job(h, 4)
                z_job(h, 5)

            norm_vector(dve)
            dve.wait_ge(rms, NHALF)
            dve.wait_ge(zeroed, 2)
            for hf in range(NHALF):
                cols = slice(hf * HALF, (hf + 1) * HALF)
                dve.wait_ge(tile, hf + 1)
                dve.tensor_tensor(mem.ab[:, cols], mem.ps[:, hf, :], mem.R[:, cols], ALU.mult).then_inc(kept, 1)
            steps(dve, step)

        @block.tensor
        def _(pe):
            def job(h, k, m, s):
                ready(pe, m, s)
                for hf in range(NHALF):
                    t = 2 * (1 + k) + hf
                    wait(pe, kept, 12 * h + t - 3)
                    in_tile(pe, mem, s, hf, t % 4).then_inc(tile, 1)

            def turn(h, e):
                _, what, n = TURNS[e]
                if what == "tok":
                    pe.wait_ge(silu, 6 * h + n + 1)
                    source = act_in[n % 2]
                else:
                    pe.wait_ge(normed, 2 * h + n + 1)
                    source = tok[n]
                for b in range(2):
                    wait(pe, held, 12 * h + 2 * e + b - 3)
                    for q in range(4):
                        c = 4 * b + q
                        last = pe.transpose(mem.ps[:, 4 + 2 * (e % 2) + b, q * P:(q + 1) * P],
                                            source[:, c * P:(c + 1) * P], mem.ident[:, :])
                    last.then_inc(turned, 1)

            def step(h):
                for k in range(6):
                    job(h, k, *use(h, k))
                    for e, (after, what, n) in enumerate(TURNS):
                        if after == k:
                            turn(h, e)

            norm_tensor(pe)
            job(0, -1, 0, 0)
            pe.wait_ge(root, NHALF)
            steps(pe, step)


def gdn_gates(nc, sems, mem):
    with ExitStack() as ctx:
        W = NV * NC

        def sb(name):
            return ctx.enter_context(nc.sbuf_tensor(f"gg_{name}", [P, W], F32))

        a, b, mag, y, u, ln, one, ea = (sb(n) for n in ("a", "b", "mag", "y", "u", "ln", "one", "ea"))
        done = sems("gg_vector")
        half_done = sems("gg_softplus")
        acted = sems("gg_scalar")
        summed = sems("gg_tensor")
        gate = {n: mem.gates[:, k, :] for k, n in enumerate(GATES)}
        G_READY = 11
        block = ctx.enter_context(nc.Block())

        def by_head(ap):
            return ap.rearrange("p c h -> p h c")

        def halves(ap):
            return ap.rearrange("p (h c) -> p h c", c=NC)

        @block.tensor
        def _(pe):
            for c in range(NC):
                last = pe.transpose(mem.ps[:, 0, c * 2 * NV:(c + 1) * 2 * NV], mem.ab[0:2 * NV, c * P:(c + 1) * P],
                                    mem.ident[0:2 * NV, 0:2 * NV])
            last.then_inc(summed, 1)
            pe.wait_ge(done, G_READY)
            pe.matmul(mem.ps[:, 1, 0:W], mem.upper[:, :], gate["g"], start=True, stop=True)
            pe.matmul(mem.ps[:, 2, 0:W], mem.ones[:, :], gate["g"], start=True, stop=True).then_inc(summed, 1)

        @block.scalar
        def _(act):
            act.activation(ea[:, 0:NV], mem.alog[:, :], ACT.Exp).then_inc(acted, 1)
            act.wait_ge(done, 2)
            act.activation(gate["beta"], b[:, :], ACT.Sigmoid).then_inc(acted, 1)
            act.wait_ge(done, 3)
            act.activation(y[:, :], mag[:, :], ACT.Exp, scale=-1.0).then_inc(acted, 1)
            act.wait_ge(done, 4)
            act.activation(ln[:, :], u[:, :], ACT.Ln).then_inc(acted, 1)
            act.wait_ge(done, G_READY + 3)
            act.activation(gate["eg"], gate["neg_gc"], ACT.Exp, scale=-1.0).then_inc(acted, 1)
            act.activation(mag[:, :], u[:, :], ACT.Exp).then_inc(acted, 1)
            act.activation(gate["egl"], one[:, :], ACT.Exp).then_inc(acted, 1)

        @block.vector
        def _(dve):
            n = 0

            def chain(instruction):
                nonlocal n
                n += 1
                instruction.then_inc(done, 1)
                dve.wait_ge(done, n)

            dve.wait_ge(summed, 1)
            ab = mem.ps[:, 0, 0:NC * 2 * NV].rearrange("p (c r) -> p c r", c=NC)
            chain(dve.tensor_tensor(halves(a[:, :]), by_head(ab[:, :, 0:NV]),
                                    mem.dtb[:, :].unsqueeze(2).to_broadcast([P, NV, NC]), ALU.add))
            chain(dve.tensor_copy(halves(b[:, :]), by_head(ab[:, :, NV:2 * NV])))
            chain(dve.scalar_tensor_tensor(out=mag[:, :], in0=a[:, :], scalar=-1.0, in1=a[:, :],
                                           op0=ALU.mult, op1=ALU.max))
            dve.wait_ge(acted, 3)
            chain(dve.tensor_scalar(u[:, :], y[:, :], 1.0, None, ALU.add))
            chain(dve.tensor_scalar(one[:, :], u[:, :], 1.0, None, ALU.is_equal))
            chain(dve.scalar_tensor_tensor(out=b[:, :], in0=u[:, :], scalar=-1.0, in1=one[:, :],
                                           op0=ALU.add, op1=ALU.add))
            chain(dve.reciprocal(b[:, :], b[:, :]))
            dve.wait_ge(acted, 4)
            chain(dve.tensor_tensor(ln[:, :], ln[:, :], one[:, :], ALU.add))
            chain(dve.tensor_tensor(ln[:, :], ln[:, :], b[:, :], ALU.mult))
            chain(dve.tensor_tensor(ln[:, :], ln[:, :], y[:, :], ALU.mult))
            n11 = n
            dve.scalar_tensor_tensor(out=ln[:, :], in0=a[:, :], scalar=0.0, in1=ln[:, :],
                                     op0=ALU.max, op1=ALU.add).then_inc(half_done, 1)
            dve.wait_ge(half_done, 1)
            assert n11 == G_READY - 1
            chain(dve.scalar_tensor_tensor(out=halves(gate["g"]), in0=halves(ln[:, :]), scalar=-1.0,
                                           in1=ea[:, 0:NV].unsqueeze(2).to_broadcast([P, NV, NC]),
                                           op0=ALU.mult, op1=ALU.mult))
            dve.wait_ge(summed, 2)
            chain(dve.tensor_scalar(gate["neg_gc"], mem.ps[:, 1, 0:W], -1.0, None, ALU.mult))
            chain(dve.tensor_copy(one[:, :], mem.ps[:, 2, 0:W]))
            chain(dve.tensor_tensor(u[:, :], one[:, :], gate["neg_gc"], ALU.add))
            dve.wait_ge(acted, 7)
            chain(dve.tensor_scalar(gate["neg_eg"], gate["eg"], -1.0, None, ALU.mult))
            chain(dve.tensor_tensor(gate["beta_ekd"], gate["beta"], mag[:, :], ALU.mult))


def turns_of_step():
    solve = []
    for g in range(GROUPS):
        solve += [("decay", g), ("products", g)]
    solve += [("turn_l", g) for g in range(GROUPS)]
    for level in range(1, LEVELS):
        for g in range(GROUPS):
            solve += [("left", g, level), ("turn_t", g, level)]
        solve += [("right", g, level) for g in range(GROUPS)]
    rest = []
    for c in range(NC):
        rest += [("state", c), ("solved", c), ("update", c)]
    merged = []
    todo = list(rest)
    gap = 0
    for n, entry in enumerate(solve):
        merged.append(entry)
        if n % 2 and todo:
            merged.append(todo.pop(0))
        elif not todo:
            gap += 1
            if gap == 2:
                merged.append(("norm",))
            if 12 <= gap and (gap - 12) % 3 == 0 and (gap - 12) // 3 < 4:
                merged.append(("turn_o", (gap - 12) // 3))
    merged += [("out", t) for t in range(2 * KT)]
    return solve, merged


GROUPS = 4
UNITS = 2 * NC
SCALAR_FILLS = ("turn_l", "turn_t")


def gdn_mix(nc, sems, mem, io):
    tag = "gm"
    SOLVE, ORDER = turns_of_step()
    FILLS = len(SOLVE)
    assert FILLS % 3 == 0
    fill_no = {e: n for n, e in enumerate(SOLVE)}
    by_scalar = [e for e in SOLVE if e[0] in SCALAR_FILLS]
    by_vector = [e for e in SOLVE if e[0] not in SCALAR_FILLS]
    ev_no = {e: n for part in (by_scalar, by_vector) for n, e in enumerate(part)}
    NA_, NV_ = len(by_scalar), len(by_vector)
    with ExitStack() as ctx:
        def sb(name, shape, dt=F32):
            return ctx.enter_context(nc.sbuf_tensor(f"{tag}_{name}", shape, dt))

        kT, qT, k_tok = (sb(n, [P, 2, SEQ]) for n in ("kT", "qT", "k"))
        v = sb("v", [P, 2, 2, SEQ])
        TT = sb("TT", [P, 2, UNITS, P])
        attn = sb("attn", [P, 2, UNITS, P])
        cur = sb("cur", [P, 2, len(GATES), 2 * NC])
        LN = sb("LN", [P, UNITS, P])
        L = sb("L", [P, UNITS, P])
        T = sb("T", [P, UNITS, P])
        ug = sb("ug", [P, 2, 4, P])
        Dg = sb("Dg", [P, 2, 4, P])
        S = sb("S", [P, 2 * DV])
        r, qs, vd, vn = (sb(n, [P, 2 * DV]) for n in ("r", "qs", "vd", "vn"))
        junk = sb("junk", [P, DV])
        ssq = sb("ssq", [P, 2 * NC])
        z = sb("z", [P, 2, SEQ])
        mem.ah, mem.al = sb("ah", [P, 2, SEQ], F32R), sb("al", [P, 2, SEQ], F32R)

        load_w, split_hi, split_lo, ready, _ = build_weight_stream(sems, mem, tag)
        inputs_in = [sems(f"{tag}_inputs_in{p}") for p in range(2)]
        z_in = sems(f"{tag}_z_in")
        gates_in = sems(f"{tag}_gates_in")
        ug_in = sems(f"{tag}_ug_in")
        start_t = sems(f"{tag}_start_t")
        fill = sems(f"{tag}_fill")
        ev_a = sems(f"{tag}_ev_a")
        ev_v = sems(f"{tag}_ev_v")
        decayed = sems(f"{tag}_decayed")
        rec = sems(f"{tag}_rec")
        r_made = sems(f"{tag}_r")
        s_made = sems(f"{tag}_s")
        o_made = sems(f"{tag}_o")
        qs_made = sems(f"{tag}_qs")
        vn_made = sems(f"{tag}_vn")
        squared = sems(f"{tag}_squared")
        o_rms = sems(f"{tag}_o_rms")
        o_inv = sems(f"{tag}_o_inv")
        o_normed = sems(f"{tag}_o_normed")
        last = sems(f"{tag}_last")
        taken = sems(f"{tag}_taken")
        a_hi = sems(f"{tag}_a_hi")
        a_lo = sems(f"{tag}_a_lo")
        block = ctx.enter_context(nc.Block())

        LAST = 4 + 2 * KT

        def steps(engine, step):
            step(0, 0, True, False)
            step(1, 1, True, True)
            with engine.Fori(1, NK // 2) as i:
                step(2 * i, 0, True, True)
                step(2 * i + 1, 1, True, True)
            step(NK, 0, False, True)

        def unit(buffer, p, u):
            return buffer[:, p, u, :]

        def group(buffer, g):
            return buffer[:, 4 * g:4 * g + 4, :]

        def bank(number):
            return mem.ps[:, number, :]

        def quad(ap):
            return ap.rearrange("p (u n) -> p u n", u=4)

        def solve_bank(entry):
            return bank(fill_no[entry] % 3)

        def bank_free(pe, h, entry):
            n = fill_no[entry] - 3
            back, before = (0, SOLVE[n]) if n >= 0 else (1, SOLVE[n + FILLS])
            if before[0] in SCALAR_FILLS:
                wait(pe, ev_a, NA_ * (h - back) + ev_no[before] + 1)
            else:
                wait(pe, ev_v, NV_ * (h - back) + ev_no[before] + 1)

        def vector_done(engine, h, entry):
            engine.wait_ge(ev_v, NV_ * h + ev_no[entry] + 1)

        def scalar_done(engine, h, entry):
            engine.wait_ge(ev_a, NA_ * h + ev_no[entry] + 1)

        def filled(engine, h, entry):
            engine.wait_ge(fill, FILLS * h + fill_no[entry] + 1)

        def gate(p, name, hh, c):
            col = hh * NC + c
            return cur[:, p, GATES.index(name), col:col + 1]

        w_out = io.gdn_w_out[0]

        @block.sync
        def _(sp):
            def head_inputs(h, p, m):
                for name, dst in (("kT", kT[:, p, :]), ("qT", qT[:, p, :]), ("k", k_tok[:, p, :])):
                    sp.dma_start(dst, mem.dram[name][bass.ds(h, 1), :, :].rearrange("o p n -> (o p) n"))\
                        .then_inc(inputs_in[p], 16)
                sp.dma_start(v[:, p, :, :], mem.dram["v"][bass.ds(2 * h, 2), :, :].rearrange("o p n -> p o n"))\
                    .then_inc(inputs_in[p], 16)

            def output_inputs(h):
                wait_before_address(sp, a_lo, 2 * h)
                sp.dma_start(z[:, :, :], mem.dram["z"][bass.ds(2 * h, 2), :, :].rearrange("o p n -> p o n"))\
                    .then_inc(z_in, 16)
                for o in range(2):
                    load_w(sp, h, o, w_out[bass.ds(2 * P * h, 2 * P), o * HALF:(o + 1) * HALF]
                           .rearrange("(k p) n -> p k n", p=P))

            def after(h, p, m):
                wait_before_address(sp, last, LAST * h + 4)
                head_inputs(h + 2, p, m + 1)
                output_inputs(h + 1)

            head_inputs(0, 0, 0)
            head_inputs(1, 1, 0)
            output_inputs(0)
            after(0, 0, 0)
            after(1, 1, 0)
            with sp.Fori(1, NK // 2 - 1) as i:
                after(2 * i, 0, i)
                after(2 * i + 1, 1, i)
            wait_before_address(sp, last, LAST * (NK - 2) + 4)
            output_inputs(NK - 1)

        @block.gpsimd
        def _(pool):
            def step(h, p, solve, rest):
                g_of = h - 1
                if solve:
                    wait(pool, last, LAST * (h - 2) + 4 if not (isinstance(h, int) and h < 2) else 0)
                    pool.tensor_copy(cur[:, p, :, :], mem.gates[:, :, bass.ds(2 * NC * h, 2 * NC)])\
                        .then_inc(gates_in, 1)
                    pool.wait_ge(gates_in, h + 1)
                for entry in ORDER:
                    if entry[0] == "decay" and solve:
                        g = entry[1]
                        if g >= 2:
                            filled(pool, h, ("decay", g - 2))
                        elif not (isinstance(h, int) and h == 0):
                            filled(pool, h - 1, ("decay", g + 2))
                        cols = cur[:, p, GATES.index("g"), :].rearrange("p (h c) -> p c h", c=NC)[:, 2 * g:2 * g + 2, :]
                        for cc in range(2):
                            w = pool.tensor_tensor(
                                ug[:, g % 2, 2 * cc:2 * cc + 2, :],
                                mem.upper[:, :].unsqueeze(1).to_broadcast([P, 2, P]),
                                cols[:, cc, :].unsqueeze(2).to_broadcast([P, 2, P]), ALU.mult)
                        w.then_inc(ug_in, 1)
                    elif entry[0] == "turn_l" and solve:
                        g = entry[1]
                        vector_done(pool, h, ("products", g))
                        dst = TT[:, p, 4 * g:4 * g + 4, :]
                        pool.tensor_tensor(dst, group(LN, g), mem.mask[0][:, :].unsqueeze(1)
                                           .to_broadcast([P, 4, P]), ALU.mult).then_inc(start_t, 1)
                        pool.wait_ge(start_t, 8 * h + 2 * g + 1)
                        pool.tensor_tensor(dst, mem.ident[:, :].unsqueeze(1).to_broadcast([P, 4, P]), dst,
                                           ALU.subtract).then_inc(start_t, 1)
                    elif entry == ("turn_o", 0) and rest:
                        for o in range(2):
                            split_lo(pool, g_of, o)
                    elif entry == ("out", 0) and rest:
                        for hh in range(2):
                            pool.wait_ge(a_hi, 2 * g_of + hh + 1)
                            pool.tensor_tensor(mem.al[:, hh, :], z[:, hh, :], mem.ah[:, hh, :].bitcast(F32),
                                               ALU.subtract).then_inc(a_lo, 1)

            steps(pool, step)

        @block.scalar
        def _(act):
            def squares(f, pf, c):
                act.wait_ge(o_made, NC * f + c + 1)
                for hh in range(2):
                    wait(act, squared, 2 * (NC * f + c) + hh)
                    act.activation(junk[:, :], v[:, pf, hh, c * DV:(c + 1) * DV], ACT.Square,
                                   accum_out=ssq[:, hh * NC + c:hh * NC + c + 1]).then_inc(squared, 1)

            def step(h, p, solve, rest):
                f, pf = h - 1, 1 - p
                for entry in ORDER:
                    kind = entry[0]
                    if kind in SCALAR_FILLS and solve:
                        g = entry[1]
                        filled(act, h, entry)
                        dst = group(L if kind == "turn_l" else T, g)
                        act.activation(dst, quad(solve_bank(entry)), ACT.Copy).then_inc(ev_a, 1)
                    elif kind == "decay" and solve:
                        g = entry[1]
                        vector_done(act, h, entry)
                        act.wait_ge(gates_in, h + 1)
                        for x in range(4):
                            c, hh = 2 * g + x // 2, x % 2
                            w = act.activation(Dg[:, g % 2, x, :], Dg[:, g % 2, x, :], ACT.Exp,
                                               bias=gate(p, "neg_gc", hh, c))
                        w.then_inc(decayed, 1)
                    elif kind == "state" and rest:
                        c = entry[1]
                        act.wait_ge(rec, 4 * (NC * f + c) + 2)
                        wait(act, o_made, NC * f + c)
                        for hh in range(2):
                            w = act.activation(qs[:, hh * DV:(hh + 1) * DV], mem.ps[:, 4, hh * DV:(hh + 1) * DV],
                                               ACT.Copy, scale=gate(pf, "eg", hh, c))
                        w.then_inc(qs_made, 1)
                    elif kind == "solved" and rest:
                        c = entry[1]
                        act.wait_ge(rec, 4 * (NC * f + c) + 3)
                        for name, dst in (("beta_ekd", vd), ("beta", vn)):
                            for hh in range(2):
                                w = act.activation(dst[:, hh * DV:(hh + 1) * DV],
                                                   mem.ps[:, 3, hh * DV:(hh + 1) * DV], ACT.Copy,
                                                   scale=gate(pf, name, hh, c))
                        w.then_inc(vn_made, 1)
                        if c >= 1:
                            squares(f, pf, c - 1)
                    elif kind == "norm" and rest:
                        squares(f, pf, NC - 1)
                        act.wait_ge(squared, 2 * NC * (f + 1))
                        act.activation(ssq[:, :], ssq[:, :], ACT.Sqrt, scale=1.0 / DV,
                                       bias=mem.eps[:, 0:1]).then_inc(o_rms, 1)
                        for o in range(2):
                            split_hi(act, f, o, last, 0 if isinstance(f, int) and f == 0 else LAST * f)
                    elif entry == ("out", 0) and rest:
                        for hh in range(2):
                            act.wait_ge(taken, LAST * f + 2 * hh + 2)
                            act.activation(mem.ah[:, hh, :], z[:, hh, :], ACT.Copy).then_inc(a_hi, 1)

            steps(act, step)

        @block.vector
        def _(dve):
            def step(h, p, solve, rest):
                f, pf = h - 1, 1 - p
                if rest:
                    wait(dve, rec, 4 * NC * f)
                    dve.memset(S[:, :], 0.0).then_inc(s_made, 1)
                for entry in ORDER:
                    kind = entry[0]
                    if kind == "decay" and solve:
                        g = entry[1]
                        filled(dve, h, entry)
                        if g >= 2:
                            vector_done(dve, h, ("products", g - 2))
                        elif not (isinstance(h, int) and h == 0):
                            vector_done(dve, h - 1, ("products", g + 2))
                        dve.tensor_tensor(Dg[:, g % 2, :, :], quad(solve_bank(entry)),
                                          mem.neg[:, :].unsqueeze(1).to_broadcast([P, 4, P]),
                                          ALU.add).then_inc(ev_v, 1)
                    elif kind == "products" and solve:
                        g = entry[1]
                        filled(dve, h, entry)
                        dve.wait_ge(decayed, GROUPS * h + g + 1)
                        ps = solve_bank(entry)
                        for x in range(4):
                            c, hh = 2 * g + x // 2, x % 2
                            dve.scalar_tensor_tensor(out=LN[:, 4 * g + x, :], in0=ps[:, (x // 2) * 256:(x // 2) * 256 + P],
                                                     scalar=gate(p, "beta", hh, c), in1=Dg[:, g % 2, x, :],
                                                     op0=ALU.mult, op1=ALU.mult)
                        for cc in range(2):
                            w = dve.tensor_tensor(attn[:, p, 4 * g + 2 * cc:4 * g + 2 * cc + 2, :],
                                                  ps[:, cc * 256 + P:cc * 256 + 2 * P].unsqueeze(1)
                                                  .to_broadcast([P, 2, P]),
                                                  Dg[:, g % 2, 2 * cc:2 * cc + 2, :], ALU.mult)
                        w.then_inc(ev_v, 1)
                    elif kind == "left" and solve:
                        _, g, level = entry
                        filled(dve, h, entry)
                        dve.tensor_tensor(group(LN, g), quad(solve_bank(entry)),
                                          mem.mask[level][:, :].unsqueeze(1).to_broadcast([P, 4, P]),
                                          ALU.mult).then_inc(ev_v, 1)
                    elif kind == "right" and solve:
                        _, g, level = entry
                        filled(dve, h, entry)
                        dst = TT[:, p, 4 * g:4 * g + 4, :]
                        dve.scalar_tensor_tensor(out=dst.rearrange("p u n -> p (u n)"), in0=solve_bank(entry),
                                                 scalar=-1.0, in1=dst.rearrange("p u n -> p (u n)"),
                                                 op0=ALU.mult, op1=ALU.add).then_inc(ev_v, 1)
                    elif kind == "state" and rest:
                        c = entry[1]
                        dve.wait_ge(rec, 4 * (NC * f + c) + 1)
                        for hh in range(2):
                            w = dve.scalar_tensor_tensor(out=r[:, hh * DV:(hh + 1) * DV],
                                                         in0=mem.ps[:, 3, hh * DV:(hh + 1) * DV],
                                                         scalar=gate(pf, "neg_eg", hh, c),
                                                         in1=v[:, pf, hh, c * DV:(c + 1) * DV],
                                                         op0=ALU.mult, op1=ALU.add)
                        w.then_inc(r_made, 1)
                    elif kind == "update" and rest:
                        c = entry[1]
                        dve.wait_ge(rec, 4 * (NC * f + c) + 4)
                        dve.wait_ge(s_made, (NC + 1) * f + c + 1)
                        for hh in range(2):
                            cols = slice(hh * DV, (hh + 1) * DV)
                            w = dve.scalar_tensor_tensor(out=S[:, cols], in0=S[:, cols],
                                                         scalar=gate(pf, "egl", hh, c), in1=mem.ps[:, 5, cols],
                                                         op0=ALU.mult, op1=ALU.add)
                        w.then_inc(s_made, 1)
                        dve.wait_ge(qs_made, NC * f + c + 1)
                        dve.wait_ge(r_made, NC * f + c + 1)
                        dve.tensor_tensor(v[:, pf, :, c * DV:(c + 1) * DV],
                                          mem.ps[:, 5, 2 * DV:4 * DV].rearrange("p (h d) -> p h d", h=2),
                                          qs[:, :].rearrange("p (h d) -> p h d", h=2), ALU.add).then_inc(o_made, 1)
                    elif kind == "norm" and rest:
                        dve.wait_ge(o_rms, f + 1)
                        dve.reciprocal(ssq[:, :], ssq[:, :]).then_inc(o_inv, 1)
                        dve.wait_ge(o_inv, f + 1)
                        for hh in range(2):
                            o = v[:, pf, hh, :].rearrange("p (c d) -> p c d", c=NC)
                            dve.tensor_tensor(o, o, ssq[:, hh * NC:(hh + 1) * NC].unsqueeze(2)
                                              .to_broadcast([P, NC, DV]), ALU.mult).then_inc(o_normed, 1)
                    elif kind == "turn_o" and rest:
                        n = entry[1]
                        dve.wait_ge(last, LAST * f + n + 1)
                        dve.wait_ge(z_in, 16 * f + 16)
                        dst = z[:, n // 2, (n % 2) * HALF:(n % 2 + 1) * HALF]
                        dve.scalar_tensor_tensor(out=dst, in0=bank(6 + n % 2), scalar=mem.par[:, 64:65], in1=dst,
                                                 op0=ALU.mult, op1=ALU.mult).then_inc(taken, 1)
                    elif kind == "out" and rest:
                        t = entry[1]
                        dve.wait_ge(last, LAST * f + 4 + t + 1)
                        dst = mem.x[:, t // 2, (t % 2) * HALF:(t % 2 + 1) * HALF]
                        dve.tensor_tensor(dst, bank(6 + t % 2), dst, ALU.add).then_inc(taken, 1)

            steps(dve, step)

        @block.tensor
        def _(pe):
            def step(h, p, solve, rest):
                f, pf = h - 1, 1 - p
                m = h // 2 if isinstance(h, int) else None
                for entry in ORDER:
                    kind = entry[0]
                    if kind == "decay" and solve:
                        g = entry[1]
                        bank_free(pe, h, entry)
                        pe.wait_ge(ug_in, GROUPS * h + g + 1)
                        pe.matmul(solve_bank(entry), mem.ones[:, :],
                                  ug[:, g % 2, :, :].rearrange("p u n -> p (u n)"),
                                  start=True, stop=True).then_inc(fill, 1)
                    elif kind == "products" and solve:
                        g = entry[1]
                        bank_free(pe, h, entry)
                        if g == 0:
                            pe.wait_ge(inputs_in[p], 64 + 64 * m if m is not None else 32 * (h - p) + 64)
                        ps = solve_bank(entry)
                        for cc in range(2):
                            tokens = slice((2 * g + cc) * C, (2 * g + cc + 1) * C)
                            pe.matmul(ps[:, cc * 256:cc * 256 + P], kT[:, p, tokens], kT[:, p, tokens],
                                      start=True, stop=True)
                            w = pe.matmul(ps[:, cc * 256 + P:cc * 256 + 2 * P], kT[:, p, tokens],
                                          qT[:, p, tokens], start=True, stop=True)
                        w.then_inc(fill, 1)
                    elif kind == "turn_l" and solve:
                        g = entry[1]
                        bank_free(pe, h, entry)
                        vector_done(pe, h, ("products", g))
                        for x in range(4):
                            w = pe.transpose(solve_bank(entry)[:, x * P:(x + 1) * P], LN[:, 4 * g + x, :],
                                             mem.ident[:, :])
                        w.then_inc(fill, 1)
                    elif kind == "left" and solve:
                        _, g, level = entry
                        bank_free(pe, h, entry)
                        if level == 1:
                            scalar_done(pe, h, ("turn_l", g))
                            pe.wait_ge(start_t, 8 * h + 2 * g + 2)
                        else:
                            vector_done(pe, h, ("right", g, level - 1))
                        for x in range(4):
                            w = pe.matmul(solve_bank(entry)[:, x * P:(x + 1) * P], L[:, 4 * g + x, :],
                                          unit(TT, p, 4 * g + x), start=True, stop=True)
                        w.then_inc(fill, 1)
                    elif kind == "turn_t" and solve:
                        _, g, level = entry
                        bank_free(pe, h, entry)
                        for x in range(4):
                            w = pe.transpose(solve_bank(entry)[:, x * P:(x + 1) * P], unit(TT, p, 4 * g + x),
                                             mem.ident[:, :])
                        w.then_inc(fill, 1)
                    elif kind == "right" and solve:
                        _, g, level = entry
                        bank_free(pe, h, entry)
                        vector_done(pe, h, ("left", g, level))
                        scalar_done(pe, h, ("turn_t", g, level))
                        for x in range(4):
                            w = pe.matmul(solve_bank(entry)[:, x * P:(x + 1) * P], T[:, 4 * g + x, :],
                                          LN[:, 4 * g + x, :], start=True, stop=True)
                        w.then_inc(fill, 1)
                    elif kind == "state" and rest:
                        c = entry[1]
                        tokens = slice(c * C, (c + 1) * C)
                        pe.wait_ge(s_made, (NC + 1) * f + c + 1)
                        wait(pe, vn_made, NC * f + c)
                        pe.matmul(mem.ps[:, 3, 0:2 * DV], kT[:, pf, tokens], S[:, :], start=True,
                                  stop=True).then_inc(rec, 1)
                        wait(pe, qs_made, NC * f + c)
                        pe.matmul(mem.ps[:, 4, 0:2 * DV], qT[:, pf, tokens], S[:, :], start=True,
                                  stop=True).then_inc(rec, 1)
                    elif kind == "solved" and rest:
                        c = entry[1]
                        pe.wait_ge(r_made, NC * f + c + 1)
                        if c == 0:
                            vector_done(pe, f, ("right", GROUPS - 1, LEVELS - 1))
                        for hh in range(2):
                            cols = slice(hh * DV, (hh + 1) * DV)
                            w = pe.matmul(mem.ps[:, 3, cols], unit(TT, pf, 2 * c + hh), r[:, cols],
                                          start=True, stop=True)
                        w.then_inc(rec, 1)
                    elif kind == "update" and rest:
                        c = entry[1]
                        pe.wait_ge(vn_made, NC * f + c + 1)
                        wait(pe, o_made, NC * f + c)
                        pe.matmul(mem.ps[:, 5, 0:2 * DV], k_tok[:, pf, c * DK:(c + 1) * DK], vd[:, :],
                                  start=True, stop=True)
                        for hh in range(2):
                            w = pe.matmul(mem.ps[:, 5, (2 + hh) * DV:(3 + hh) * DV], unit(attn, pf, 2 * c + hh),
                                          vn[:, hh * DV:(hh + 1) * DV], start=True, stop=True)
                        w.then_inc(rec, 1)
                    elif kind == "turn_o" and rest:
                        n = entry[1]
                        pe.wait_ge(o_normed, 2 * f + n // 2 + 1)
                        wait(pe, taken, LAST * f + n - 1)
                        for q in range(4):
                            c = 4 * (n % 2) + q
                            w = pe.transpose(bank(6 + n % 2)[:, q * P:(q + 1) * P],
                                             v[:, pf, n // 2, c * DV:(c + 1) * DV], mem.ident[:, :])
                        w.then_inc(last, 1)
                    elif kind == "out" and rest:
                        t = entry[1]
                        if t == 0:
                            pe.wait_ge(a_lo, 2 * f + 2)
                        if t % 8 == 0:
                            ready(pe, f, t // 8)
                        wait(pe, taken, LAST * f + 4 + t - 1)
                        out_tile(pe, mem, t // 8, (t // 2) % 4, t % 2, 6 + t % 2).then_inc(last, 1)

            steps(pe, step)


def phase_finish(nc, sems, mem, io):
    with ExitStack() as ctx:
        y = ctx.enter_context(nc.sbuf_tensor("fin_y", [P, KT, SEQ], F32))
        rows = ctx.enter_context(nc.sbuf_tensor("fin_rows", [P, NC, D], F32))
        mem.sq = ctx.enter_context(nc.sbuf_tensor("fin_sq", [P, 2, SEQ], F32))
        mem.R = ctx.enter_context(nc.sbuf_tensor("fin_R", [P, SEQ], F32))
        sq = sems("fin_sq")
        summed = sems("fin_summed")
        root = sems("fin_root")
        rms = sems("fin_rms")
        normed = sems("fin_normed")
        turned = sems("fin_turned")
        kept_v = sems("fin_kept_v")
        kept_a = sems("fin_kept_a")
        stored = sems("fin_stored")
        block = ctx.enter_context(nc.Block())

        @block.sync
        def _(sp):
            for c in range(NC):
                sp.wait_ge(kept_v, c + 1)
                sp.wait_ge(kept_a, c + 1)
                sp.dma_start(io.out[0, c * P:(c + 1) * P, :], rows[:, c, :]).then_inc(stored, 16)
            sp.wait_ge(stored, 16 * NC)

        @block.scalar
        def _(act):
            for m in range(KT):
                wait(act, summed, m - 1)
                act.activation(mem.sq[:, m % 2, :], mem.x[:, m, :], ACT.Square).then_inc(sq, 1)
            act.wait_ge(summed, KT)
            for hf in range(NHALF):
                act.activation(mem.R[:, hf * HALF:(hf + 1) * HALF], mem.ps[:, 4 + hf, :], ACT.Sqrt,
                               scale=1.0 / D, bias=mem.eps[:, 0:1]).then_inc(root, 1)
            for c in range(NC):
                act.wait_ge(turned, 2 * c + 2)
                act.activation(rows[:, c, HALF:D], mem.ps[:, (2 * c + 1) % 8, :], ACT.Copy).then_inc(kept_a, 1)

        @block.vector
        def _(dve):
            for hf in range(NHALF):
                dve.wait_ge(root, hf + 1)
                dve.reciprocal(mem.R[:, hf * HALF:(hf + 1) * HALF],
                               mem.R[:, hf * HALF:(hf + 1) * HALF]).then_inc(rms, 1)
            dve.wait_ge(rms, NHALF)
            for m in range(KT):
                dve.scalar_tensor_tensor(out=y[:, m, :], in0=mem.x[:, m, :], scalar=mem.par[:, 32 + m:33 + m],
                                         in1=mem.R[:, :], op0=ALU.mult, op1=ALU.mult).then_inc(normed, 1)
            for c in range(NC):
                dve.wait_ge(turned, 2 * c + 1)
                dve.tensor_copy(rows[:, c, 0:HALF], mem.ps[:, (2 * c) % 8, :]).then_inc(kept_v, 1)

        @block.tensor
        def _(pe):
            for m in range(KT):
                pe.wait_ge(sq, m + 1)
                for hf in range(NHALF):
                    last = pe.matmul(mem.ps[:, 4 + hf, :], mem.ones[:, :],
                                     mem.sq[:, m % 2, hf * HALF:(hf + 1) * HALF],
                                     start=(m == 0), stop=(m == KT - 1))
                last.then_inc(summed, 1)
            pe.wait_ge(normed, KT)
            pe.wait_ge(root, NHALF)
            for c in range(NC):
                for g in range(2):
                    t = 2 * c + g
                    wait(pe, (kept_v, kept_a)[g], c - 3)
                    for q in range(4):
                        last = pe.transpose(mem.ps[:, t % 8, q * P:(q + 1) * P],
                                            y[:, 4 * g + q, c * P:(c + 1) * P], mem.ident[:, :])
                    last.then_inc(turned, 1)


class Names:
    pass


def build(nc, io, phases=("sc", "ffn0", "gdn", "ffn1")):
    mem = Names()
    with ExitStack() as ctx:
        def sb(name, shape, dt=F32):
            return ctx.enter_context(nc.sbuf_tensor(name, shape, dt))

        def sems(name):
            return ctx.enter_context(nc.semaphore(name))

        mem.par_rows = {"par": 65, "ffn": 2 * FFN_TAPS * 2 * FT}
        mem.x = sb("x_res", [P, KT, SEQ])
        mem.raw = sb("w_raw", [P, 2, WCOLS])
        mem.wh = [sb(f"w_hi{s}", [P, WCOLS], F32R) for s in range(2)]
        mem.wl = [sb(f"w_lo{s}", [P, WCOLS], F32R) for s in range(2)]
        mem.ident, mem.ones, mem.eps = sb("ident", [P, P]), sb("ones", [P, P]), sb("eps", [P, 1])
        mem.par = sb("par", [P, mem.par_rows["par"]])
        mem.fcw = sb("ffn_taps", [P, mem.par_rows["ffn"]])
        mem.gcw = sb("gdn_taps", [P, P])
        mem.alog, mem.dtb = sb("a_log", [P, NV]), sb("dt_bias", [P, NV])
        mem.ps = ctx.enter_context(nc.psum_tensor("ps", [P, 8, HALF], F32))
        phase_load(nc, sems, mem, io)
        if "sc" in phases:
            phase_mix(nc, sems, mem, io, "sc", 0)
        if "ffn0" in phases:
            phase_mix(nc, sems, mem, io, "ffn", 0)
        if "gdn" in phases:
            phase_gdn(nc, sems, mem, io)
        if "ffn1" in phases:
            phase_mix(nc, sems, mem, io, "ffn", 1)
        phase_finish(nc, sems, mem, io)


INPUTS = ["x", "norm_mix", "norm_ffn", "sc_w_in", "sc_conv", "sc_w_out", "gdn_w_in", "gdn_conv", "gdn_a_log",
          "gdn_dt_bias", "gdn_norm", "gdn_w_out", "ffn_w_up", "ffn_conv", "ffn_w_down", "norm_final"]


def kernel(**inputs):
    import numpy as np
    import concourse.bacc as bacc
    from concourse.bass_utils import run_bass_kernel_spmd

    nc = bacc.Bacc("TRN2", target_bir_lowering=False, num_devices=1)
    io, arrays = Names(), {}
    for name in INPUTS:
        a = np.ascontiguousarray(inputs[name])
        arrays[f"in_{name}"] = a
        io.__dict__[name] = nc.dram_tensor(f"in_{name}", a.shape, F32, kind="ExternalInput").ap()
    io.out = nc.dram_tensor("out", [1, SEQ, D], F32, kind="ExternalOutput").ap()
    build(nc, io)
    result = run_bass_kernel_spmd(nc, [arrays], core_ids=[0])
    return result.results[0]["out"]
```

```python
import concourse.bass as bass
from concourse import mybir
from contextlib import ExitStack

F32 = mybir.dt.float32
F32R = mybir.dt.float32r
ALU = mybir.AluOpType
ACT = mybir.ActivationFunctionType
AX = mybir.AxisListType

P = 128
SEQ = 1024
D = 1024
KT = D // P
HALF = 512
NHALF = SEQ // HALF
EPS = 1e-6
SC_TAPS = 3
NK, NV, DK, DV = 8, 16, 128, 128
GDN_TAPS = 4
QKV = 2 * NK * DK + NV * DV
QKV_T = QKV // P
GPROJ = QKV + NV * DV + 2 * NV
D_FF = 2816
FT = D_FF // P
FFN_TAPS = 3
C = 128
NC = SEQ // C
BIG = 1e30
WCOLS = 1024


def wait(engine, semaphore, value):
    if not isinstance(value, int) or value > 0:
        engine.wait_ge(semaphore, value)


def wait_before_address(sp, semaphore, value):
    if not isinstance(value, int) or value > 0:
        sp.wait_ge(semaphore, value)
        sp.nop(nofuse=True)


def first_weights(io, phase):
    if phase == "gdn":
        w_in, ab = io.gdn_w_in[0].rearrange("(k p) n -> p k n", p=P), QKV + NV * DV
        return [(slice(0, 2 * NV), w_in[:, :, ab:GPROJ]), (slice(2 * NV, P), w_in[:, :, 0:P - 2 * NV])]
    w_up = io.sc_w_in[0] if phase == "sc" else io.ffn_w_up[int(phase[-1])]
    start = D if phase == "sc" else 0
    return [(slice(0, P), w_up.rearrange("(k p) n -> p k n", p=P)[:, :, start:start + P])]


def prefetch(sp, mem):
    if mem.first_jobs:
        for columns, source in mem.first_jobs.pop(0):
            sp.dma_start(mem.raw[:, 0, :].rearrange("p (k n) -> p k n", k=KT)[:, :, columns],
                         source).then_inc(mem.first_in, 16)
            mem.first_count += 16


def build_weight_stream(sems, mem, tag, prefetched=True):
    first_count = mem.first_count
    w_in = [sems(f"{tag}_w_in{s}") for s in range(2)]
    w_hi = sems(f"{tag}_w_hi")
    w_lo = sems(f"{tag}_w_lo")

    def load(sp, m, s, src):
        wait_before_address(sp, w_lo, 2 * m + s - 1)
        width = src.shape[1] * src.shape[2]
        sp.dma_start(mem.raw[:, s, 0:width].rearrange("p (k n) -> p k n", k=src.shape[1]),
                     src).then_inc(w_in[s], 16)

    def split_hi(act, m, s, done, value):
        if not prefetched or s == 1:
            act.wait_ge(w_in[s], 16 * m + 16)
        elif isinstance(m, int) and m == 0:
            act.wait_ge(mem.first_in, first_count)
        else:
            act.wait_ge(w_in[s], 16 * m)
        wait(act, done, value)
        act.activation(mem.wh[s][:, :], mem.raw[:, s, :], ACT.Copy).then_inc(w_hi, 1)

    def split_lo(pool, m, s):
        pool.wait_ge(w_hi, 2 * m + s + 1)
        pool.tensor_tensor(mem.wl[s][:, :], mem.raw[:, s, :], mem.wh[s][:, :].bitcast(F32),
                           ALU.subtract).then_inc(w_lo, 1)

    def ready(pe, m, s):
        pe.wait_ge(w_lo, 2 * m + s + 1)

    def all_split(sp, m, s):
        sp.wait_ge(w_lo, 2 * m + s + 1)
        prefetch(sp, mem)

    return load, split_hi, split_lo, ready, all_split


def products(pe, out, pairs, begin=True, end=True):
    last = None
    for k, (wh, wl, ah, al) in enumerate(pairs):
        pe.matmul(out, wh, ah, start=(begin and k == 0), stop=False)
        pe.matmul(out, wh, al, start=False, stop=False)
        last = pe.matmul(out, wl, ah, start=False, stop=(end and k == len(pairs) - 1))
    return last


def in_tile(pe, mem, s, hf, bank):
    cols = slice(hf * HALF, (hf + 1) * HALF)
    return products(pe, mem.ps[:, bank, :],
                    [(mem.wh[s][:, k * P:(k + 1) * P], mem.wl[s][:, k * P:(k + 1) * P],
                      mem.xh[:, k, cols], mem.xl[:, k, cols]) for k in range(KT)])


def out_tile(pe, mem, s, m, hf, bank, ks=(0, 1)):
    cols = slice(hf * HALF, (hf + 1) * HALF)
    return products(pe, mem.ps[:, bank, :],
                    [(mem.wh[s][:, k * 512 + m * P:k * 512 + (m + 1) * P],
                      mem.wl[s][:, k * 512 + m * P:k * 512 + (m + 1) * P],
                      mem.ah[:, k, cols], mem.al[:, k, cols]) for k in ks], 0 in ks, 1 in ks)


def build_norm(sems, mem, gain, tag):
    hi = sems(f"{tag}_x_hi")
    sq = sems(f"{tag}_x_sq")
    lo = sems(f"{tag}_x_lo")
    added = sems(f"{tag}_x_added")
    summed = sems(f"{tag}_x_sum")
    root = sems(f"{tag}_x_root")
    rms = sems(f"{tag}_x_rms")

    def scalar(act, split_hi, tile):
        split_hi(act, 0, 0, tile, 0)
        for m in range(KT):
            act.activation(mem.xh[:, m, :], mem.x[:, m, :], ACT.Copy,
                           scale=mem.par[:, gain + m:gain + m + 1]).then_inc(hi, 1)
        split_hi(act, 0, 1, tile, 0)
        for m in range(KT):
            if m >= 3:
                act.wait_ge(added, m - 2)
            act.activation(mem.R[:, :] if m == 0 else mem.sq[:, m % 2, :], mem.x[:, m, :],
                           ACT.Square).then_inc(sq, 1)
        split_hi(act, 1, 0, tile, 2)
        act.wait_ge(summed, 1)
        for hf in range(NHALF):
            act.activation(mem.R[:, hf * HALF:(hf + 1) * HALF], mem.ps[:, 4 + hf, :], ACT.Sqrt,
                           scale=1.0 / D, bias=mem.eps[:, 0:1]).then_inc(root, 1)

    def vector(dve):
        for m in range(KT):
            dve.wait_ge(hi, m + 1)
            dve.scalar_tensor_tensor(out=mem.xl[:, m, :], in0=mem.x[:, m, :],
                                     scalar=mem.par[:, gain + m:gain + m + 1],
                                     in1=mem.xh[:, m, :].bitcast(F32),
                                     op0=ALU.mult, op1=ALU.subtract).then_inc(lo, 1)
        for m in range(1, KT):
            dve.wait_ge(sq, m + 1)
            if m >= 2:
                dve.wait_ge(added, m - 1)
            dve.tensor_tensor(mem.R[:, :], mem.R[:, :], mem.sq[:, m % 2, :], ALU.add).then_inc(added, 1)

    def inverse(dve, hf):
        dve.wait_ge(root, hf + 1)
        dve.reciprocal(mem.R[:, hf * HALF:(hf + 1) * HALF],
                       mem.R[:, hf * HALF:(hf + 1) * HALF]).then_inc(rms, 1)
        dve.wait_ge(rms, hf + 1)

    def first_job(pe, ready, tile):
        ready(pe, 0, 0)
        for k in range(KT):
            pe.wait_ge(lo, k + 1)
            wh, wl = (w[0][:, k * P:(k + 1) * P] for w in (mem.wh, mem.wl))
            for hf in range(NHALF):
                cols, out = slice(hf * HALF, (hf + 1) * HALF), mem.ps[:, hf, :]
                pe.matmul(out, wh, mem.xh[:, k, cols], start=(k == 0), stop=False)
                pe.matmul(out, wh, mem.xl[:, k, cols], start=False, stop=False)
                last = pe.matmul(out, wl, mem.xh[:, k, cols], start=False, stop=(k == KT - 1))
                if k == KT - 1:
                    last.then_inc(tile, 1)

    def sums(pe):
        pe.wait_ge(added, KT - 1)
        for hf in range(NHALF):
            last = pe.matmul(mem.ps[:, 4 + hf, :], mem.ones[:, :], mem.R[:, hf * HALF:(hf + 1) * HALF],
                             start=True, stop=True)
        last.then_inc(summed, 1)

    return scalar, vector, inverse, first_job, sums


def phase_load(nc, sems, mem, io):
    with ExitStack() as ctx:
        stage = ctx.enter_context(nc.sbuf_tensor("stage", [P, NC, D], F32))
        pstage = ctx.enter_context(nc.sbuf_tensor("pstage", [P, 5, P], F32))
        x_in = [sems(f"load_x_in{hf}") for hf in range(NHALF)]
        p_in = sems("load_p_in")
        made = sems("load_const")
        turned = sems("load_turned")
        kept_v = sems("load_kept_v")
        kept_a = sems("load_kept_a")
        block = ctx.enter_context(nc.Block())
        rows = mem.par_rows

        def x_tile(t):
            return mem.x[:, t % KT, (t // KT) * HALF:(t // KT + 1) * HALF]

        def count_of(t):
            return t + 1 if t < KT else t + 3

        ffn_rows = rows["ffn"] // 3

        @block.sync
        def _(sp):
            for c in range(NC):
                sp.dma_start(stage[:, c, :], io.x[0, c * P:(c + 1) * P, :])\
                    .then_inc(x_in[c // 4], 16)
            prefetch(sp, mem)

        @block.scalar
        def _(act):
            act.dma_start(pstage[0:16, 0, :], io.norm_mix.rearrange("l (m p) -> (l m) p", p=P)).then_inc(p_in, 16)
            act.dma_start(pstage[16:32, 0, :], io.norm_ffn.rearrange("l (m p) -> (l m) p", p=P)).then_inc(p_in, 16)
            act.dma_start(pstage[32:40, 0, :], io.norm_final.rearrange("(m p) -> m p", p=P)).then_inc(p_in, 16)
            act.dma_start(pstage[40:64, 0, :], io.sc_conv.rearrange("l t (m p) -> (l t m) p", p=P)).then_inc(p_in, 16)
            act.dma_start(pstage[64:65, 0, :], io.gdn_norm).then_inc(p_in, 16)
            act.dma_start(pstage[:, 1, :], io.gdn_conv.rearrange("l t (m p) -> (l t m) p", p=P)).then_inc(p_in, 16)
            fc = io.ffn_conv.rearrange("l t (m p) -> (l t m) p", p=P)
            for g in range(3):
                act.dma_start(pstage[0:ffn_rows, 2 + g, :],
                              fc[g * ffn_rows:(g + 1) * ffn_rows, :]).then_inc(p_in, 16)
            act.dma_start(mem.alog[:, :], io.gdn_a_log.partition_broadcast(P)).then_inc(p_in, 16)
            act.dma_start(mem.dtb[:, :], io.gdn_dt_bias.partition_broadcast(P)).then_inc(p_in, 16)
            act.wait_ge(p_in, 16 * 11)
            for t in range(1, 2 * KT, 2):
                act.wait_ge(turned, count_of(t))
                act.activation(x_tile(t), mem.ps[:, t % 8, :], ACT.Copy).then_inc(kept_a, 1)

        @block.gpsimd
        def _(pool):
            pool.memset(mem.ones[:, :], 1.0).then_inc(made, 1)
            pool.memset(mem.ident[:, :], 0.0).then_inc(made, 1)
            pool.memset(mem.eps[:, :], EPS).then_inc(made, 1)
            pool.wait_ge(made, 2)
            pool.affine_select(out=mem.ident[:, :], in_=mem.ident[:, :], compare_op=ALU.not_equal, fill=1.0,
                               base=0, pattern=[[-1, P]], channel_multiplier=1).then_inc(made, 1)

        @block.vector
        def _(dve):
            for t in range(0, 2 * KT, 2):
                if t == KT:
                    dve.wait_ge(turned, KT + 1)
                    dve.tensor_copy(mem.par[:, :], mem.ps[:, 0, 0:rows["par"]]).then_inc(kept_v, 1)
                    dve.tensor_copy(mem.gcw[:, :], mem.ps[:, 0, P:2 * P]).then_inc(kept_v, 1)
                    dve.wait_ge(turned, KT + 2)
                    dve.tensor_copy(mem.fcw[:, :], mem.ps[:, 1, 0:rows["ffn"]]).then_inc(kept_v, 1)
                dve.wait_ge(turned, count_of(t))
                dve.tensor_copy(x_tile(t), mem.ps[:, t % 8, :]).then_inc(kept_v, 1)

        @block.tensor
        def _(pe):
            def parameters():
                pe.wait_ge(p_in, 16 * 11)
                pe.wait_ge(kept_v, 1)
                pe.transpose(mem.ps[:, 0, 0:rows["par"]], pstage[0:rows["par"], 0, :],
                             mem.ident[0:rows["par"], 0:rows["par"]])
                pe.transpose(mem.ps[:, 0, P:2 * P], pstage[:, 1, :], mem.ident[:, :]).then_inc(turned, 1)
                pe.wait_ge(kept_a, 1)
                for g in range(3):
                    last = pe.transpose(mem.ps[:, 1, g * ffn_rows:(g + 1) * ffn_rows],
                                        pstage[0:ffn_rows, 2 + g, :], mem.ident[0:ffn_rows, 0:ffn_rows])
                last.then_inc(turned, 1)

            pe.wait_ge(made, 4)
            for t in range(2 * KT):
                if t == KT:
                    parameters()
                if t % KT == 0:
                    pe.wait_ge(x_in[t // KT], 16 * NC // 2)
                if t in (KT, KT + 1):
                    pe.wait_ge(kept_v, KT // 2 + 2 + t - KT)
                elif t > KT:
                    pe.wait_ge((kept_v, kept_a)[t % 2], (t - KT) // 2 + 1)
                for q in range(4):
                    c = (t // KT) * 4 + q
                    last = pe.transpose(mem.ps[:, t % 8, q * P:(q + 1) * P],
                                        stage[:, c, (t % KT) * P:(t % KT + 1) * P], mem.ident[:, :])
                last.then_inc(turned, 1)


def convolve(dve, dst, src, taps, tap, base):
    last = len(taps) - 1
    dve.tensor_scalar(dst, src[:, last:last + SEQ], taps[last], None, ALU.mult).then_inc(tap, 1)
    for n, k in enumerate(reversed(range(last))):
        dve.wait_ge(tap, base + n + 1)
        dve.scalar_tensor_tensor(out=dst, in0=src[:, k:k + SEQ], scalar=taps[k], in1=dst,
                                 op0=ALU.mult, op1=ALU.add).then_inc(tap, 1)


def phase_mix(nc, sems, mem, io, kind, layer):
    ffn = kind == "ffn"
    tag = f"{kind}{layer}"
    R = 2 if ffn else 3
    U = 2 * R
    STEPS = (FT if ffn else KT) // 2
    TILES = 2 * U + 16
    PAD = 2
    w_up = (io.ffn_w_up[layer] if ffn else io.sc_w_in[0]).rearrange("(k p) n -> p k n", p=P)
    w_down = io.ffn_w_down[layer] if ffn else io.sc_w_out[0]
    with ExitStack() as ctx:
        def sb(name, shape, dt=F32):
            return ctx.enter_context(nc.sbuf_tensor(f"{tag}_{name}", shape, dt))

        mem.xh, mem.xl = sb("xh", [P, KT, SEQ], F32R), sb("xl", [P, KT, SEQ], F32R)
        mem.ah, mem.al = sb("ah", [P, 2, SEQ], F32R), sb("al", [P, 2, SEQ], F32R)
        mem.sq, mem.R = sb("sq", [P, 2, SEQ]), sb("R", [P, SEQ])
        padded = [sb(f"pad{b}", [P, PAD + SEQ]) for b in range(2)]
        conved = sb("conved", [P, SEQ])
        hidden = sb("hidden", [P, SEQ])
        scratch = None if ffn else sb("scratch", [P, SEQ])
        cgate = None if ffn else sb("cgate", [P, SEQ])

        load, split_hi, split_lo, ready, all_split = build_weight_stream(sems, mem, tag)
        norm_scalar, norm_vector, norm_inverse, first_job, norm_sums = build_norm(
            sems, mem, (16 if ffn else 0) + 8 * layer, tag)
        zeroed = sems(f"{tag}_zeroed")
        tile = sems(f"{tag}_tile")
        kept = sems(f"{tag}_kept")
        product = sems(f"{tag}_product")
        tap = sems(f"{tag}_tap")
        silu = sems(f"{tag}_silu")
        gated = sems(f"{tag}_gated")
        a_hi = sems(f"{tag}_a_hi")
        a_lo = sems(f"{tag}_a_lo")
        added = sems(f"{tag}_added")
        block = ctx.enter_context(nc.Block())

        def ups(last):
            return U - 1 if last else U

        def use(i, q):
            return ((U + 2) // 2) * i + (1 + q) // 2, (1 + q) % 2

        def tiles_before(i, q, last):
            return TILES * i + 2 + 2 * min(q, ups(last)) + 8 * max(0, q - ups(last))

        def up_src(i, k):
            f, r = (1 + k) // R, (1 + k) % R
            part = (0, D_FF)[r] if ffn else (D, 2 * D, 0)[r]
            return w_up[:, :, bass.ds(2 * P * i + (f * P + part), P)]

        def down_src(i, o):
            return w_down[bass.ds(2 * P * i, 2 * P), o * HALF:(o + 1) * HALF].rearrange("(k p) n -> p k n", p=P)

        def steps(engine, step):
            step(0, False)
            with engine.Fori(1, STEPS - 1) as i:
                step(i, False)
            step(STEPS - 1, True)

        @block.sync
        def _(sp):
            def step(i, last):
                for q in range(ups(last) + 2):
                    src = up_src(i, q) if q < ups(last) else down_src(i, q - ups(last))
                    load(sp, *use(i, q), src)

            steps(sp, step)
            all_split(sp, *use(STEPS - 1, ups(True) + 1))

        @block.gpsimd
        def _(pool):
            for b in range(2):
                pool.memset(padded[b][:, 0:PAD], 0.0).then_inc(zeroed, 1)

            def step(i, last):
                for q in range(ups(last) + 2):
                    if q < ups(last) + 1:
                        split_lo(pool, *use(i, q + 1))
                    elif not last:
                        split_lo(pool, *use(i, q + 1))
                    if q < U and q % R == R - 1:
                        f = q // R
                        pool.wait_ge(a_hi, 2 * i + f + 1)
                        pool.tensor_tensor(mem.al[:, f, :], hidden[:, :], mem.ah[:, f, :].bitcast(F32),
                                           ALU.subtract).then_inc(a_lo, 1)

            split_lo(pool, 0, 0)
            split_lo(pool, 0, 1)
            steps(pool, step)

        @block.scalar
        def _(act):
            def step(i, last):
                for q in range(ups(last) + 2):
                    first = isinstance(i, int) and i == 0 and q == 0
                    if (q < ups(last) + 1 or not last) and not first:
                        split_hi(act, *use(i, q + 1), tile, tiles_before(i, q, last))
                    f = q // R
                    if ffn and q < U and q % R == 0:
                        act.wait_ge(tap, 6 * (2 * i + f) + 3)
                        act.activation(conved[:, :], conved[:, :], ACT.Silu).then_inc(silu, 1)
                    if q < U and q % R == R - 1:
                        act.wait_ge(gated, 2 * i + f + 1)
                        wait(act, tile, TILES * i + 2 if f == 0 and not (isinstance(i, int) and i == 0) else 0)
                        act.activation(mem.ah[:, f, :], hidden[:, :], ACT.Copy).then_inc(a_hi, 1)

            norm_scalar(act, split_hi, tile)
            steps(act, step)

        @block.vector
        def _(dve):
            def keep(i, k, hf, dst):
                cols = slice(hf * HALF, (hf + 1) * HALF)
                t = 2 * (1 + k) + hf
                if k == -1 and isinstance(i, int) and i == 0:
                    norm_inverse(dve, hf)
                dve.wait_ge(tile, TILES * i + t + 1)
                dve.tensor_tensor(dst, mem.ps[:, t % 4, :], mem.R[:, cols], ALU.mult).then_inc(kept, 1)

            def kept_both(i, k):
                dve.wait_ge(kept, 2 * U * i + 2 * (1 + k) + 2)

            def ffn_job(i, k):
                r, f = (1 + k) % R, (1 + k) // R
                u = U * i + (1 + k)
                wait(dve, tap, 3 * u - 3)
                for hf in range(NHALF):
                    keep(i, k, hf, padded[r][:, PAD + hf * HALF:PAD + (hf + 1) * HALF])
                kept_both(i, k)
                taps = [mem.fcw[:, bass.ds((layer * FFN_TAPS + j) * 2 * FT + r * FT + 2 * i + f, 1)]
                        for j in range(FFN_TAPS)]
                if r == 0:
                    wait(dve, gated, 2 * i + f)
                    convolve(dve, conved[:, :], padded[0], taps, tap, 3 * u)
                else:
                    wait(dve, a_lo, 2 * i + f)
                    convolve(dve, hidden[:, :], padded[1], taps, tap, 3 * u)
                    dve.wait_ge(tap, 3 * u + 3)
                    dve.wait_ge(silu, 2 * i + f + 1)
                    dve.tensor_tensor(hidden[:, :], hidden[:, :], conved[:, :], ALU.mult).then_inc(gated, 1)

            def sc_job(i, k):
                r, f = (1 + k) % R, (1 + k) // R
                if r == 0:
                    wait(dve, product, 2 * i + f)
                    for hf in range(NHALF):
                        keep(i, k, hf, cgate[:, hf * HALF:(hf + 1) * HALF])
                elif r == 1:
                    wait(dve, gated, 2 * i + f)
                    for hf in range(NHALF):
                        keep(i, k, hf, scratch[:, hf * HALF:(hf + 1) * HALF])
                    kept_both(i, k)
                    wait(dve, tap, 3 * (2 * i + f))
                    dve.tensor_tensor(padded[0][:, PAD:PAD + SEQ], scratch[:, :], cgate[:, :],
                                      ALU.mult).then_inc(product, 1)
                    dve.wait_ge(product, 2 * i + f + 1)
                    convolve(dve, conved[:, :], padded[0],
                             [mem.par[:, bass.ds(40 + 8 * j + 2 * i + f, 1)] for j in range(SC_TAPS)],
                             tap, 3 * (2 * i + f))
                else:
                    dve.wait_ge(product, 2 * i + f + 1)
                    for hf in range(NHALF):
                        keep(i, k, hf, scratch[:, hf * HALF:(hf + 1) * HALF])
                    kept_both(i, k)
                    dve.wait_ge(tap, 3 * (2 * i + f) + 3)
                    wait(dve, a_lo, 2 * i + f)
                    dve.tensor_tensor(hidden[:, :], conved[:, :], scratch[:, :], ALU.mult).then_inc(gated, 1)

            def step(i, last):
                for k in range(ups(last)):
                    (ffn_job if ffn else sc_job)(i, k)
                for t in range(2 * KT):
                    dve.wait_ge(tile, tiles_before(i, ups(last), last) + t + 1)
                    cols = slice((t % 2) * HALF, (t % 2 + 1) * HALF)
                    dve.tensor_tensor(mem.x[:, t // 2, cols], mem.ps[:, 4 + t % 4, :], mem.x[:, t // 2, cols],
                                      ALU.add).then_inc(added, 1)

            norm_vector(dve)
            dve.wait_ge(zeroed, 2)
            (ffn_job if ffn else sc_job)(0, -1)
            steps(dve, step)

        @block.tensor
        def _(pe):
            def up_job(i, k, m, s):
                ready(pe, m, s)
                for hf in range(NHALF):
                    t = 2 * (1 + k) + hf
                    wait(pe, kept, 2 * U * i + t - 3)
                    in_tile(pe, mem, s, hf, t % 4).then_inc(tile, 1)
                    if isinstance(i, int) and t == 2 and i == 0:
                        norm_sums(pe)

            def step(i, last):
                for k in range(ups(last)):
                    up_job(i, k, *use(i, k))
                begun = 0
                if last:
                    pe.wait_ge(a_lo, 2 * i + 1)
                    m, s = use(i, ups(last))
                    ready(pe, m, s)
                    begun = 4
                    for t in range(begun):
                        wait(pe, added, 16 * i + t - 3)
                        out_tile(pe, mem, s, (t // 2) % 4, t % 2, 4 + t % 4, ks=(0,))
                pe.wait_ge(a_lo, 2 * i + 2)
                for o in range(2):
                    m, s = use(i, ups(last) + o)
                    ready(pe, m, s)
                    for t in range(8 * o, 8 * o + 8):
                        wait(pe, added, 16 * i + t - 3)
                        out_tile(pe, mem, s, (t // 2) % 4, t % 2, 4 + t % 4,
                                 ks=(1,) if t < begun else (0, 1)).then_inc(tile, 1)

            first_job(pe, ready, tile)
            steps(pe, step)


def phase_gdn(nc, sems, mem, io):
    with ExitStack() as ctx:
        def sb(name, shape, dt=F32):
            return ctx.enter_context(nc.sbuf_tensor(f"gdn_{name}", shape, dt))

        mem.gates = sb("gates", [P, len(GATES), NV * NC])
        mem.ab = sb("ab", [P, SEQ])
        mem.upper = sb("upper", [P, P])
        mem.neg = sb("neg", [P, P])
        mem.mask = {l: sb(f"mask{l}", [P, P]) for l in LEVELS if l != TOP}
        mem.dram = {name: nc.dram_tensor(f"scratch_{name}", shape, F32).ap()
                    for name, shape in (("qT", [NK, P, SEQ]), ("kT", [NK, P, SEQ]), ("k", [NK, P, SEQ]),
                                        ("v", [NV, P, SEQ]), ("z", [NV, P, SEQ]),
                                        ("blocks", [NB, UNITS, BLOCK, BLOCK]),
                                        ("inverses", [NB, UNITS, BLOCK, BLOCK]))}
        gdn_project(nc, sems, mem, io)
        gdn_mix(nc, sems, mem, io)


GATES = ("g", "beta", "neg_gc", "eg", "neg_eg", "beta_ekd", "egl")
BLOCK = 16
NB = C // BLOCK
LEVELS = range(4, 7)
TOP = LEVELS[-1]
assert 1 << LEVELS[0] == BLOCK and 2 << TOP == C


def make_masks(pool, mem, made):
    n = 0
    for m, value in [(mem.upper, 1.0), (mem.neg, 0.0)] + [(m, 1.0) for m in mem.mask.values()]:
        pool.memset(m[:, :], value).then_inc(made, 1)
        n += 1
    pool.wait_ge(made, n)
    pool.affine_select(out=mem.upper[:, :], in_=mem.upper[:, :], compare_op=ALU.is_ge, fill=0.0, base=0,
                       pattern=[[1, P]], channel_multiplier=-1).then_inc(made, 1)
    pool.affine_select(out=mem.neg[:, :], in_=mem.neg[:, :], compare_op=ALU.is_ge, fill=-BIG, base=0,
                       pattern=[[1, P]], channel_multiplier=-1).then_inc(made, 1)
    n += 2
    for l, mask in mem.mask.items():
        s = 1 << l
        view = mask[:, :].rearrange("p (b r) -> p b r", r=2 * s)
        blocks = P // (2 * s)
        for base, channel, pattern in ((0, 1, [[-2 * s, blocks], [0, 2 * s]]),
                                       (s - 1, -1, [[2 * s, blocks], [0, 2 * s]]),
                                       (-s, 0, [[0, blocks], [1, 2 * s]])):
            pool.affine_select(out=view, in_=view, compare_op=ALU.is_ge, fill=0.0, base=base,
                               pattern=pattern, channel_multiplier=channel).then_inc(made, 1)
            n += 1
            pool.wait_ge(made, n)


def gdn_project(nc, sems, mem, io):
    tag = "gp"
    PAD = GDN_TAPS - 1
    w_in = io.gdn_w_in[0].rearrange("(k p) n -> p k n", p=P)
    with ExitStack() as ctx:
        def sb(name, shape, dt=F32):
            return ctx.enter_context(nc.sbuf_tensor(f"{tag}_{name}", shape, dt))

        mem.R = sb("R", [P, SEQ])
        mem.xh, mem.xl = sb("xh", [P, KT, SEQ], F32R), sb("xl", [P, KT, SEQ], F32R)
        padded = [sb(f"pad{b}", [P, PAD + SEQ]) for b in range(2)]
        act_in = [sb(f"conved{b}", [P, SEQ]) for b in range(2)]
        mem.sq = sb("sq", [P, 2, SEQ])
        tok = [sb(f"tok{e}", [P, SEQ]) for e in range(4)]
        back = [sb(f"back{e}", [P, SEQ]) for e in range(2)]
        zbuf = [sb(f"z{e}", [P, SEQ]) for e in range(2)]
        inv = [sb(f"inv{e}", [P, NC]) for e in range(2)]
        qeps = sb("qeps", [P, 2])

        load, split_hi, split_lo, ready, _ = build_weight_stream(sems, mem, tag)
        norm_scalar, norm_vector, norm_inverse, first_job, norm_sums = build_norm(sems, mem, 8, tag)
        gates_tensor, gates_scalar, gates_vector = build_gates(sems, mem, sb)
        made = sems(f"{tag}_made")
        zeroed = sems(f"{tag}_zeroed")
        tile = sems(f"{tag}_tile")
        kept = sems(f"{tag}_kept")
        tap = sems(f"{tag}_tap")
        silu = sems(f"{tag}_silu")
        turned = sems(f"{tag}_turned")
        held = sems(f"{tag}_held")
        square = sems(f"{tag}_square")
        norm2 = sems(f"{tag}_norm2")
        norm = sems(f"{tag}_norm")
        inverse = sems(f"{tag}_inverse")
        normed = sems(f"{tag}_normed")
        stored = {b: sems(f"{tag}_stored_{b}") for b in ("back0", "back1", "tok1", "tok2", "tok3", "z0", "z1")}
        block = ctx.enter_context(nc.Block())

        TURNS = ((1, "tok", 0), (2, "tok", 1), (3, "tok", 2), (4, "tok", 3), (4, "back", 0), (5, "back", 1))

        def use(h, k):
            return 3 * h + (1 + k) // 2, (1 + k) % 2

        def src(h, k):
            base = (0, NK * DK, 2 * NK * DK, 2 * NK * DK + DV, QKV, QKV + DV)[k]
            return w_in[:, :, bass.ds(h * (P if k < 2 else 2 * P) + base, P)]

        def steps(engine, step):
            step(0)
            with engine.Fori(1, NK) as h:
                step(h)

        @block.sync
        def _(sp):
            def store(h, k):
                def put(name, buffer, index, key):
                    sp.dma_start(mem.dram[name][bass.ds(index, 1), :, :].rearrange("o p n -> (o p) n"),
                                 buffer[:, :]).then_inc(stored[key], 16)
                if k == 0:
                    wait_before_address(sp, held, 12 * h + 10)
                    put("qT", back[0], h, "back0")
                elif k == 1:
                    wait_before_address(sp, normed, 2 * h + 2)
                    put("k", tok[1], h, "tok1")
                    wait_before_address(sp, held, 12 * h + 12)
                    put("kT", back[1], h, "back1")
                elif k in (2, 3):
                    wait_before_address(sp, held, 12 * h + (6 if k == 2 else 8))
                    put("v", tok[k], 2 * h + k - 2, f"tok{k}")
                else:
                    wait_before_address(sp, silu, 6 * h + k + 1)
                    put("z", zbuf[k - 4], 2 * h + k - 4, f"z{k - 4}")

            for k in range(6):
                load(sp, *use(0, k), src(0, k))
            with sp.Fori(1, NK) as h:
                for k in range(6):
                    load(sp, *use(h, k), src(h, k))
                    store(h - 1, k)
            for k in range(6):
                store(NK - 1, k)
            for key in stored:
                sp.wait_ge(stored[key], 16 * NK)

        @block.gpsimd
        def _(pool):
            for b in range(2):
                pool.memset(padded[b][:, 0:PAD], 0.0).then_inc(zeroed, 1)
            pool.memset(qeps[:, 0:1], EPS * DK).then_inc(zeroed, 1)
            pool.memset(qeps[:, 1:2], EPS).then_inc(zeroed, 1)
            split_lo(pool, 0, 0)
            split_lo(pool, 0, 1)
            make_masks(pool, mem, made)

            for k in range(6):
                split_lo(pool, *use(0, k + 1))
            with pool.Fori(1, NK - 1) as h:
                for k in range(6):
                    split_lo(pool, *use(h, k + 1))
            for k in range(5):
                split_lo(pool, *use(NK - 1, k + 1))

        @block.scalar
        def _(act):
            def hold(h, e, b):
                _, what, n = TURNS[e]
                act.wait_ge(turned, 12 * h + 2 * e + b + 1)
                if b == 0 and not (isinstance(h, int) and h == 0):
                    key = f"{what}{n}"
                    if key in stored:
                        act.wait_ge(stored[key], 16 * h)
                dst = (tok if what == "tok" else back)[n]
                act.activation(dst[:, b * HALF:(b + 1) * HALF], mem.ps[:, 4 + 2 * (e % 2) + b, :],
                               ACT.Copy).then_inc(held, 1)

            def root_of(h, e):
                act.wait_ge(norm2, 2 * h + e + 1)
                act.activation(inv[e][:, :], inv[e][:, :], ACT.Sqrt, scale=float(DK) if e == 0 else 1.0,
                               bias=qeps[:, e:e + 1]).then_inc(norm, 1)

            def step(h, last):
                for k in range(6):
                    if (k < 5 or not last) and not (isinstance(h, int) and h == 0 and k == 0):
                        split_hi(act, *use(h, k + 1), tile, 2 * (6 * h + k) + 2)
                    if k >= 1:
                        do_silu(h, k - 1)
                    if k == 4:
                        root_of(h, 0)
                        root_of(h, 1)
                    for e, (after, what, n) in enumerate(TURNS):
                        if after == k:
                            hold(h, e, 0)
                            hold(h, e, 1)
                    if isinstance(h, int) and h == 0 and k in (2, 4):
                        gates_scalar[k // 2 - 1](act)
                do_silu(h, 5)

            def do_silu(h, k):
                if k < 4:
                    act.wait_ge(tap, 16 * h + 4 * k + 4)
                    act.activation(act_in[k % 2][:, :], act_in[k % 2][:, :], ACT.Silu).then_inc(silu, 1)
                else:
                    act.wait_ge(kept, 12 * h + 2 * k + 4)
                    act.activation(zbuf[k - 4][:, :], zbuf[k - 4][:, :], ACT.Silu).then_inc(silu, 1)

            norm_scalar(act, split_hi, tile)
            act.wait_ge(zeroed, 4)
            step(0, False)
            with act.Fori(1, NK - 1) as h:
                step(h, False)
            step(NK - 1, True)
            gates_scalar[2](act)

        @block.vector
        def _(dve):
            def keep(h, k, hf, dst):
                t = 12 * h + 2 * (1 + k) + hf
                cols = slice(hf * HALF, (hf + 1) * HALF)
                dve.wait_ge(tile, t + 1)
                dve.tensor_tensor(dst, mem.ps[:, (2 * (1 + k) + hf) % 4, :], mem.R[:, cols],
                                  ALU.mult).then_inc(kept, 1)

            def conv_job(h, k):
                b = k % 2
                wait(dve, tap, 16 * h + 4 * (k - 1))
                for hf in range(NHALF):
                    keep(h, k, hf, padded[b][:, PAD + hf * HALF:PAD + (hf + 1) * HALF])
                dve.wait_ge(kept, 12 * h + 2 * (1 + k) + 2)
                if k >= 2:
                    dve.wait_ge(turned, 12 * h + 2 * (k - 2) + 2)
                elif not (isinstance(h, int) and h == 0):
                    dve.wait_ge(turned, 12 * (h - 1) + (6 if k == 0 else 8))
                first = QT[k]
                taps = [mem.gcw[:, bass.ds(j * QKV_T + first + h * (1 if k < 2 else 2), 1)]
                        for j in range(GDN_TAPS)]
                convolve(dve, act_in[b][:, :], padded[b], taps, tap, 16 * h + 4 * k)

            QT = (0, NK, 2 * NK, 2 * NK + 1)

            def sums(h, e):
                dve.wait_ge(held, 12 * h + 2 * e + 2)
                wait(dve, norm2, 2 * h + e - 1)
                dve.tensor_tensor(mem.sq[:, e, :], tok[e][:, :], tok[e][:, :], ALU.mult).then_inc(square, 1)
                dve.wait_ge(square, 2 * h + e + 1)
                wait(dve, normed, 2 * h + e - 1)
                dve.tensor_reduce(inv[e][:, :], mem.sq[:, e, :].rearrange("p (c d) -> p c d", c=NC), AX.X,
                                  ALU.add).then_inc(norm2, 1)

            def scale(h, e):
                dve.wait_ge(norm, 2 * h + e + 1)
                dve.reciprocal(inv[e][:, :], inv[e][:, :]).then_inc(inverse, 1)
                dve.wait_ge(inverse, 2 * h + e + 1)
                view = tok[e][:, :].rearrange("p (c d) -> p c d", c=NC)
                dve.tensor_tensor(view, view, inv[e][:, :].unsqueeze(2).to_broadcast([P, NC, DK]),
                                  ALU.mult).then_inc(normed, 1)

            def z_job(h, k):
                if not (isinstance(h, int) and h == 0):
                    dve.wait_ge(stored[f"z{k - 4}"], 16 * h)
                for hf in range(NHALF):
                    keep(h, k, hf, zbuf[k - 4][:, hf * HALF:(hf + 1) * HALF])

            def step(h):
                gates = gates_vector if isinstance(h, int) and h == 0 else None
                conv_job(h, 0)
                conv_job(h, 1)
                if gates:
                    gates[0](dve)
                sums(h, 0)
                conv_job(h, 2)
                sums(h, 1)
                conv_job(h, 3)
                if gates:
                    gates[1](dve)
                scale(h, 0)
                scale(h, 1)
                z_job(h, 4)
                z_job(h, 5)
                if gates:
                    gates[2](dve)

            norm_vector(dve)
            dve.wait_ge(zeroed, 2)
            for hf in range(NHALF):
                cols = slice(hf * HALF, (hf + 1) * HALF)
                norm_inverse(dve, hf)
                dve.wait_ge(tile, hf + 1)
                dve.tensor_tensor(mem.ab[:, cols], mem.ps[:, hf, :], mem.R[:, cols], ALU.mult).then_inc(kept, 1)
            steps(dve, step)
            gates_vector[3](dve)

        @block.tensor
        def _(pe):
            def job(h, k, m, s):
                ready(pe, m, s)
                for hf in range(NHALF):
                    t = 2 * (1 + k) + hf
                    wait(pe, kept, 12 * h + t - 3)
                    in_tile(pe, mem, s, hf, t % 4).then_inc(tile, 1)
                    if isinstance(h, int) and t == 2 and h == 0:
                        norm_sums(pe)

            def turn(h, e):
                _, what, n = TURNS[e]
                if what == "tok":
                    pe.wait_ge(silu, 6 * h + n + 1)
                    source = act_in[n % 2]
                else:
                    pe.wait_ge(normed, 2 * h + n + 1)
                    source = tok[n]
                for b in range(2):
                    wait(pe, held, 12 * h + 2 * e + b - 3)
                    for q in range(4):
                        c = 4 * b + q
                        last = pe.transpose(mem.ps[:, 4 + 2 * (e % 2) + b, q * P:(q + 1) * P],
                                            source[:, c * P:(c + 1) * P], mem.ident[:, :])
                    last.then_inc(turned, 1)

            def step(h):
                for k in range(6):
                    job(h, k, *use(h, k))
                    if isinstance(h, int) and h == 0 and k == 1:
                        pe.wait_ge(kept, 2)
                        gates_tensor[0](pe)
                    if isinstance(h, int) and h == 0 and k == 2:
                        gates_tensor[1](pe)
                    for e, (after, what, n) in enumerate(TURNS):
                        if after == k:
                            turn(h, e)

            first_job(pe, ready, tile)
            steps(pe, step)
            pe.wait_ge(made, 4 + 4 * len(mem.mask))
            pe.wait_ge(held, 12 * NK - 2)
            gates_tensor[2](pe)


def build_gates(sems, mem, sb):
    W = NV * NC
    a, b, mag, y, u, ln, one, ea = (sb(f"gate_{n}", [P, W]) for n in ("a", "b", "mag", "y", "u", "ln", "one", "ea"))
    done = sems("gates_vector")
    half_done = sems("gates_softplus")
    acted = sems("gates_scalar")
    summed = sems("gates_tensor")
    gate = {n: mem.gates[:, k, :] for k, n in enumerate(GATES)}
    G_READY = 11

    def by_head(ap):
        return ap.rearrange("p c h -> p h c")

    def halves(ap):
        return ap.rearrange("p (h c) -> p h c", c=NC)

    def turn_ab(pe):
        for c in range(NC):
            last = pe.transpose(mem.ps[:, 6, c * 2 * NV:(c + 1) * 2 * NV], mem.ab[0:2 * NV, c * P:(c + 1) * P],
                                mem.ident[0:2 * NV, 0:2 * NV])
        last.then_inc(summed, 1)

    def ab_left(pe):
        pe.wait_ge(done, 2)

    def sum_g(pe):
        pe.wait_ge(done, G_READY)
        pe.matmul(mem.ps[:, 4, 0:W], mem.upper[:, :], gate["g"], start=True, stop=True)
        pe.matmul(mem.ps[:, 5, 0:W], mem.ones[:, :], gate["g"], start=True, stop=True).then_inc(summed, 1)

    def exponentials(act):
        act.activation(ea[:, 0:NV], mem.alog[:, :], ACT.Exp).then_inc(acted, 1)
        act.wait_ge(done, 2)
        act.activation(gate["beta"], b[:, :], ACT.Sigmoid).then_inc(acted, 1)
        act.wait_ge(done, 3)
        act.activation(y[:, :], mag[:, :], ACT.Exp, scale=-1.0).then_inc(acted, 1)

    def logarithm(act):
        act.wait_ge(done, 4)
        act.activation(ln[:, :], u[:, :], ACT.Ln).then_inc(acted, 1)

    def decays(act):
        act.wait_ge(done, G_READY + 3)
        act.activation(gate["eg"], gate["neg_gc"], ACT.Exp, scale=-1.0).then_inc(acted, 1)
        act.activation(mag[:, :], u[:, :], ACT.Exp).then_inc(acted, 1)
        act.activation(gate["egl"], one[:, :], ACT.Exp).then_inc(acted, 1)

    n = 0

    def chain(dve, instruction):
        nonlocal n
        n += 1
        instruction.then_inc(done, 1)
        dve.wait_ge(done, n)

    def magnitudes(dve):
        dve.wait_ge(summed, 1)
        ab = mem.ps[:, 6, 0:NC * 2 * NV].rearrange("p (c r) -> p c r", c=NC)
        chain(dve, dve.tensor_tensor(halves(a[:, :]), by_head(ab[:, :, 0:NV]),
                                     mem.dtb[:, :].unsqueeze(2).to_broadcast([P, NV, NC]), ALU.add))
        chain(dve, dve.tensor_copy(halves(b[:, :]), by_head(ab[:, :, NV:2 * NV])))
        chain(dve, dve.scalar_tensor_tensor(out=mag[:, :], in0=a[:, :], scalar=-1.0, in1=a[:, :],
                                            op0=ALU.mult, op1=ALU.max))

    def guard(dve):
        dve.wait_ge(acted, 3)
        chain(dve, dve.tensor_scalar(u[:, :], y[:, :], 1.0, None, ALU.add))
        chain(dve, dve.tensor_scalar(one[:, :], u[:, :], 1.0, None, ALU.is_equal))
        chain(dve, dve.scalar_tensor_tensor(out=b[:, :], in0=u[:, :], scalar=-1.0, in1=one[:, :],
                                            op0=ALU.add, op1=ALU.add))
        chain(dve, dve.reciprocal(b[:, :], b[:, :]))

    def softplus(dve):
        dve.wait_ge(acted, 4)
        chain(dve, dve.tensor_tensor(ln[:, :], ln[:, :], one[:, :], ALU.add))
        chain(dve, dve.tensor_tensor(ln[:, :], ln[:, :], b[:, :], ALU.mult))
        chain(dve, dve.tensor_tensor(ln[:, :], ln[:, :], y[:, :], ALU.mult))
        dve.scalar_tensor_tensor(out=ln[:, :], in0=a[:, :], scalar=0.0, in1=ln[:, :],
                                 op0=ALU.max, op1=ALU.add).then_inc(half_done, 1)
        dve.wait_ge(half_done, 1)
        assert n == G_READY - 1
        chain(dve, dve.scalar_tensor_tensor(out=halves(gate["g"]), in0=halves(ln[:, :]), scalar=-1.0,
                                            in1=ea[:, 0:NV].unsqueeze(2).to_broadcast([P, NV, NC]),
                                            op0=ALU.mult, op1=ALU.mult))

    def from_sums(dve):
        dve.wait_ge(summed, 2)
        chain(dve, dve.tensor_scalar(gate["neg_gc"], mem.ps[:, 4, 0:W], -1.0, None, ALU.mult))
        chain(dve, dve.tensor_copy(one[:, :], mem.ps[:, 5, 0:W]))
        chain(dve, dve.tensor_tensor(u[:, :], one[:, :], gate["neg_gc"], ALU.add))
        dve.wait_ge(acted, 7)
        chain(dve, dve.tensor_scalar(gate["neg_eg"], gate["eg"], -1.0, None, ALU.mult))
        chain(dve, dve.tensor_tensor(gate["beta_ekd"], gate["beta"], mag[:, :], ALU.mult))

    return (turn_ab, ab_left, sum_g), (exponentials, logarithm, decays), (magnitudes, guard, softplus, from_sums)


def turns_of_step():
    solve = []
    for g in range(GROUPS):
        solve += [("decay", g), ("products", g)]
    solve += [("blocks",)] + [("turn_l", g) for g in range(GROUPS)]
    for level in LEVELS:
        for g in range(GROUPS):
            solve += [("left", g, level), ("turn_t", g, level)]
        solve += [("right", g, level) for g in range(GROUPS)]
    rec = []
    for c in range(NC):
        rec += [("state", c), ("solved", c), ("update", c)]
    rec.append(("norm",))
    finish = [("turn_o", n) for n in range(4)] + [("split_o",)] + [("out", t) for t in range(2 * KT)]
    costs = {"decay": (9, 7, 11, 0), "products": (9, 20, 0, 0), "turn_l": (3, 0, 6, 0),
             "blocks": (0, 0, 0, 270), "left": (9, 7, 0, 0),
             "turn_t": (3, 0, 6, 0), "right": (9, 7, 0, 0), "state": (9, 7, 6, 0), "solved": (5, 0, 12, 0),
             "update": (9, 11, 6, 0), "norm": (0, 40, 20, 0), "turn_o": (3, 8, 0, 0),
             "split_o": (0, 0, 20, 60), "out": (13, 7, 0, 0)}
    LAG = 1
    done = {}
    pe = dve = act = pool = 0
    streams = {"rec": rec, "solve": list(solve), "finish": finish}
    order, filled = [], {"rec": [], "solve": [], "finish": []}

    def needs(name, entry):
        kind = entry[0]
        before = []
        if name == "solve":
            before = filled["solve"][-3:-2] if kind != "blocks" else [("products", GROUPS - 1)]
            if kind == "products":
                before = before + [("decay", entry[1])]
            elif kind == "turn_l":
                before = before + [("products", entry[1])]
            elif kind == "left":
                before = before + [("right", entry[1], entry[2] - 1), ("turn_l", entry[1]), ("blocks",)]
            elif kind == "turn_t":
                before = before + [("right", entry[1], entry[2] - 1), ("blocks",)]
            elif kind == "right":
                before = before + [("left", entry[1], entry[2]), ("turn_t", entry[1], entry[2])]
        elif name == "rec":
            before = filled["rec"][-1:]
        else:
            before = filled["finish"][-2:-1]
            if kind == "out" and entry[1] == 0:
                before = before + [("split_o",)]
            if kind == "split_o":
                before = [("turn_o", 3)]
        return before

    while any(streams.values()):
        best = None
        for rank, (name, left) in enumerate(streams.items()):
            if left:
                start = max([pe] + [done.get(b, 0) + LAG for b in needs(name, left[0])])
                if best is None or start < best[0]:
                    best = (start, rank, name)
        start, _, name = best
        entry = streams[name].pop(0)
        t_pe, t_dve, t_act, t_pool = costs[entry[0]]
        pe = start + t_pe
        end = pe
        if t_dve:
            dve = end = max(dve, pe) + t_dve
        if t_act:
            act = max(act, end if entry[0] == "decay" else pe) + t_act
            end = max(end, act)
        if t_pool:
            pool = end = max(pool, end) + t_pool
        done[entry] = end
        if entry[0] not in ("norm", "blocks"):
            filled[name].append(entry)
        order.append(entry)
    return [entry for entry in solve if entry != ("blocks",)], order


GROUPS = 4
UNITS = 2 * NC
SCALAR_FILLS = ("turn_l", "turn_t")


def gdn_mix(nc, sems, mem, io):
    tag = "gm"
    SOLVE, ORDER = turns_of_step()
    FILLS = len(SOLVE)
    assert FILLS % 3 == 0
    fill_no = {e: n for n, e in enumerate(SOLVE)}
    by_scalar = [e for e in SOLVE if e[0] in SCALAR_FILLS]
    by_vector = [e for e in SOLVE if e[0] not in SCALAR_FILLS]
    ev_no = {e: n for part in (by_scalar, by_vector) for n, e in enumerate(part)}
    NA_, NV_ = len(by_scalar), len(by_vector)
    with ExitStack() as ctx:
        def sb(name, shape, dt=F32):
            return ctx.enter_context(nc.sbuf_tensor(f"{tag}_{name}", shape, dt))

        kT, qT = sb("kT", [P, SEQ]), sb("qT", [P, SEQ])
        rkT, rqT, rk = (sb(n, [P, SEQ]) for n in ("rkT", "rqT", "rk"))
        v = sb("v", [P, 2, 2, SEQ])
        TT = sb("TT", [P, 2, UNITS, P])
        attn = sb("attn", [P, 2, UNITS, P])
        cur = sb("cur", [P, 2, len(GATES), 2 * NC])
        LN = sb("LN", [P, UNITS, P])
        L = sb("L", [P, UNITS, P])
        T = sb("T", [P, UNITS, P])
        Dg = sb("Dg", [P, 2, 4, P])
        S = sb("S", [P, 2 * DV])
        r, qs, vd, vn = (sb(n, [P, 2 * DV]) for n in ("r", "qs", "vd", "vn"))
        junk = sb("junk", [P, DV])
        B, Y = sb("B", [P, BLOCK, BLOCK]), sb("Y", [P, BLOCK, BLOCK])
        outer = sb("outer", [P, BLOCK * BLOCK // 2])
        eye = sb("eye", [P, BLOCK, BLOCK])
        ssq = sb("ssq", [P, 2 * NC])
        z = sb("z", [P, 2, SEQ])
        mem.ah, mem.al = sb("ah", [P, 2, SEQ], F32R), sb("al", [P, 2, SEQ], F32R)

        load_w, split_hi, split_lo, ready, all_split = build_weight_stream(sems, mem, tag, prefetched=False)
        solve_in = sems(f"{tag}_solve_in")
        rec_in = [sems(f"{tag}_rec_in{b}") for b in range(2)]
        v_in = [sems(f"{tag}_v_in{p}") for p in range(2)]
        z_in = sems(f"{tag}_z_in")
        gates_in = sems(f"{tag}_gates_in")
        blocks_out = sems(f"{tag}_blocks_out")
        blocks_in = sems(f"{tag}_blocks_in")
        eye_made = sems(f"{tag}_eye_made")
        cleared = sems(f"{tag}_cleared")
        substituted = sems(f"{tag}_substituted")
        inverses_out = sems(f"{tag}_inverses_out")
        inverses_in = sems(f"{tag}_inverses_in")
        fill = sems(f"{tag}_fill")
        ev_a = sems(f"{tag}_ev_a")
        ev_v = sems(f"{tag}_ev_v")
        decayed = sems(f"{tag}_decayed")
        rec = sems(f"{tag}_rec")
        r_made = sems(f"{tag}_r")
        s_made = sems(f"{tag}_s")
        o_made = sems(f"{tag}_o")
        qs_made = sems(f"{tag}_qs")
        vn_made = sems(f"{tag}_vn")
        squared = sems(f"{tag}_squared")
        o_rms = sems(f"{tag}_o_rms")
        o_inv = sems(f"{tag}_o_inv")
        o_normed = sems(f"{tag}_o_normed")
        last = sems(f"{tag}_last")
        taken = sems(f"{tag}_taken")
        a_hi = sems(f"{tag}_a_hi")
        a_lo = sems(f"{tag}_a_lo")
        block = ctx.enter_context(nc.Block())

        LAST = 4 + 2 * KT
        SUBST = 1 + 2 * (BLOCK - 1)

        def steps(engine, step):
            step(0, 0, True, False, False)
            step(1, 1, True, True, False)
            with engine.Fori(1, NK // 2) as i:
                step(2 * i, 0, True, True, True)
                step(2 * i + 1, 1, True, True, True)
            step(NK, 0, False, True, True)
            step(NK + 1, 1, False, False, True)

        def unit(buffer, p, u):
            return buffer[:, p, u, :]

        def group(buffer, g):
            return buffer[:, 4 * g:4 * g + 4, :]

        def bank(number):
            return mem.ps[:, number, :]

        def quad(ap):
            return ap.rearrange("p (u n) -> p u n", u=4)

        def solve_bank(entry):
            return bank(fill_no[entry] % 3)

        H = C // 2

        def quarter(entry):
            return solve_bank(entry)[0:H, 0:4 * H].rearrange("p (u n) -> p u n", u=4)

        def bank_free(pe, h, entry):
            n = fill_no[entry] - 3
            back, before = (0, SOLVE[n]) if n >= 0 else (1, SOLVE[n + FILLS])
            if before[0] in SCALAR_FILLS:
                wait(pe, ev_a, NA_ * (h - back) + ev_no[before] + 1)
            else:
                wait(pe, ev_v, NV_ * (h - back) + ev_no[before] + 1)

        def vector_done(engine, h, entry):
            engine.wait_ge(ev_v, NV_ * h + ev_no[entry] + 1)

        def scalar_done(engine, h, entry):
            engine.wait_ge(ev_a, NA_ * h + ev_no[entry] + 1)

        def filled(engine, h, entry):
            engine.wait_ge(fill, FILLS * h + fill_no[entry] + 1)

        def parity_loaded(engine, semaphore, h, p, each):
            engine.wait_ge(semaphore, each * (h // 2 + 1) if isinstance(h, int) else (each // 2) * (h - p) + each)

        def gate(p, name, hh, c):
            col = hh * NC + c
            return cur[:, p, GATES.index(name), col:col + 1]

        w_out = io.gdn_w_out[0]

        @block.sync
        def _(sp):
            def row(name, h):
                return mem.dram[name][bass.ds(h, 1), :, :].rearrange("o p n -> (o p) n")

            def solve_inputs(h):
                if not (isinstance(h, int) and h == 0):
                    wait_before_address(sp, fill, FILLS * (h - 1) + fill_no[("products", GROUPS - 1)] + 1)
                for name, dst in (("kT", kT), ("qT", qT)):
                    sp.dma_start(dst[:, :], row(name, h)).then_inc(solve_in, 16)

            def rec_inputs(h, b):
                if not (isinstance(h, int) and h == 0):
                    wait_before_address(sp, rec, 4 * NC * (h - 1) + 2 * NC * (b + 1))
                cols = slice(b * HALF, (b + 1) * HALF)
                for name, dst in (("kT", rkT), ("qT", rqT), ("k", rk)):
                    sp.dma_start(dst[:, cols], row(name, h)[:, cols]).then_inc(rec_in[b], 16)

            def v_inputs(h, p):
                if not (isinstance(h, int) and h < 2):
                    wait_before_address(sp, last, LAST * (h - 2) + 4)
                sp.dma_start(v[:, p, :, :], mem.dram["v"][bass.ds(2 * h, 2), :, :].rearrange("o p n -> p o n"))\
                    .then_inc(v_in[p], 16)

            def output_inputs(h):
                wait_before_address(sp, a_lo, 2 * h)
                sp.dma_start(z[:, :, :], mem.dram["z"][bass.ds(2 * h, 2), :, :].rearrange("o p n -> p o n"))\
                    .then_inc(z_in, 16)
                for o in range(2):
                    load_w(sp, h, o, w_out[bass.ds(2 * P * h, 2 * P), o * HALF:(o + 1) * HALF]
                           .rearrange("(k p) n -> p k n", p=P))

            def blocks_to_partitions(h):
                wait_before_address(sp, ev_v, NV_ * h + ev_no[("products", GROUPS - 1)] + 1)
                for b in range(NB):
                    rows = slice(b * BLOCK, (b + 1) * BLOCK)
                    sp.dma_start(mem.dram["blocks"][b].rearrange("u j i -> j u i"),
                                 LN[rows, :, rows]).then_inc(blocks_out, 16)
                wait_before_address(sp, blocks_out, 16 * NB * h + 16 * NB)
                sp.dma_start(B[:, :, :].rearrange("p j i -> p (j i)"),
                             mem.dram["blocks"].rearrange("b u j i -> (b u) (j i)")).then_inc(blocks_in, 16)

            def inverses_to_diagonal(h, p):
                wait_before_address(sp, substituted, SUBST * h + SUBST)
                sp.dma_start(mem.dram["inverses"].rearrange("b u j i -> (b u) (j i)"),
                             Y[:, :, :].rearrange("p j i -> p (j i)")).then_inc(inverses_out, 16)
                wait_before_address(sp, inverses_out, 16 * h + 16)
                wait_before_address(sp, cleared, h + 1)
                for b in range(NB):
                    rows = slice(b * BLOCK, (b + 1) * BLOCK)
                    sp.dma_start(TT[rows, p, :, rows],
                                 mem.dram["inverses"][b].rearrange("u j i -> j u i")).then_inc(inverses_in, 16)

            def step(h, p):
                v_inputs(h, p)
                blocks_to_partitions(h)
                if not isinstance(h, int) or h < NK - 1:
                    solve_inputs(h + 1)
                inverses_to_diagonal(h, p)
                rec_inputs(h, 0)
                if not (isinstance(h, int) and h == 0):
                    output_inputs(h - 1)
                rec_inputs(h, 1)

            solve_inputs(0)
            step(0, 0)
            step(1, 1)
            with sp.Fori(1, NK // 2 - 1) as i:
                step(2 * i, 0)
                step(2 * i + 1, 1)
            step(NK - 2, 0)
            step(NK - 1, 1)
            output_inputs(NK - 1)
            all_split(sp, NK - 1, 1)

        @block.gpsimd
        def _(pool):
            def step(h, p, solve, recur, finish):
                f = h - 2
                if solve:
                    wait(pool, o_made, NC * (h - 1) if not (isinstance(h, int) and h < 2) else 0)
                    pool.tensor_copy(cur[:, p, :, :], mem.gates[:, :, bass.ds(2 * NC * h, 2 * NC)])\
                        .then_inc(gates_in, 1)
                    pool.memset(TT[:, p, :, :], 0.0).then_inc(cleared, 1)
                for entry in ORDER:
                    kind = entry[0]
                    if kind == "blocks" and solve:
                        wait(pool, inverses_out, 16 * h)
                        pool.tensor_tensor(Y[:, :, :], eye[:, :, :], eye[:, :, :], ALU.mult).then_inc(substituted, 1)
                        pool.wait_ge(blocks_in, 16 * h + 16)
                        for k in range(BLOCK - 1):
                            i, n = BLOCK - 1 - k, k + 1
                            product = outer[:, 0:i * n].rearrange("p (j n) -> p j n", n=n)
                            pool.wait_ge(substituted, SUBST * h + 1 + 2 * k)
                            pool.tensor_tensor(product, B[:, 0:i, i].unsqueeze(2).to_broadcast([P, i, n]),
                                               Y[:, i, i:BLOCK].unsqueeze(1).to_broadcast([P, i, n]),
                                               ALU.mult).then_inc(substituted, 1)
                            pool.wait_ge(substituted, SUBST * h + 2 + 2 * k)
                            pool.tensor_tensor(Y[:, 0:i, i:BLOCK], Y[:, 0:i, i:BLOCK], product,
                                               ALU.subtract).then_inc(substituted, 1)
                    elif entry == ("turn_o", 0) and finish:
                        split_lo(pool, f, 0)
                    elif kind == "split_o" and finish:
                        for hh in range(2):
                            pool.wait_ge(a_hi, 2 * f + hh + 1)
                            pool.tensor_tensor(mem.al[:, hh, :], z[:, hh, :], mem.ah[:, hh, :].bitcast(F32),
                                               ALU.subtract).then_inc(a_lo, 1)
                        split_lo(pool, f, 1)

            flat = eye[:, :, :].rearrange("p j i -> p (j i)")
            pool.memset(flat, 0.0).then_inc(eye_made, 1)
            pool.wait_ge(eye_made, 1)
            pool.memset(flat[:, 0:BLOCK * BLOCK:BLOCK + 1], 1.0).then_inc(eye_made, 1)
            pool.wait_ge(eye_made, 2)
            steps(pool, step)

        @block.scalar
        def _(act):
            def squares(f, pf, c):
                act.wait_ge(o_made, NC * f + c + 1)
                for hh in range(2):
                    wait(act, squared, 2 * (NC * f + c) + hh)
                    act.activation(junk[:, :], v[:, pf, hh, c * DV:(c + 1) * DV], ACT.Square,
                                   accum_out=ssq[:, hh * NC + c:hh * NC + c + 1]).then_inc(squared, 1)

            def step(h, p, solve, recur, finish):
                f, pf, e = h - 1, 1 - p, h - 2
                for entry in ORDER:
                    kind = entry[0]
                    if kind in SCALAR_FILLS and solve:
                        g = entry[1]
                        filled(act, h, entry)
                        dst = group(L if kind == "turn_l" else T, g)
                        w = C // 2 if entry[-1] == TOP and kind == "turn_t" else C
                        act.activation(dst[:, :, 0:w], quad(solve_bank(entry))[:, :, 0:w],
                                       ACT.Copy).then_inc(ev_a, 1)
                    elif kind == "decay" and solve:
                        g = entry[1]
                        vector_done(act, h, entry)
                        act.wait_ge(gates_in, h + 1)
                        for x in range(4):
                            c, hh = 2 * g + x // 2, x % 2
                            w = act.activation(Dg[:, g % 2, x, :], Dg[:, g % 2, x, :], ACT.Exp,
                                               bias=gate(p, "neg_gc", hh, c))
                        w.then_inc(decayed, 1)
                    elif kind == "state" and recur:
                        c = entry[1]
                        act.wait_ge(rec, 4 * (NC * f + c) + 2)
                        wait(act, o_made, NC * f + c)
                        for hh in range(2):
                            w = act.activation(qs[:, hh * DV:(hh + 1) * DV], mem.ps[:, 4, hh * DV:(hh + 1) * DV],
                                               ACT.Copy, scale=gate(pf, "eg", hh, c))
                        w.then_inc(qs_made, 1)
                    elif kind == "solved" and recur:
                        c = entry[1]
                        act.wait_ge(rec, 4 * (NC * f + c) + 3)
                        for name, dst in (("beta_ekd", vd), ("beta", vn)):
                            for hh in range(2):
                                w = act.activation(dst[:, hh * DV:(hh + 1) * DV],
                                                   mem.ps[:, 3, hh * DV:(hh + 1) * DV], ACT.Copy,
                                                   scale=gate(pf, name, hh, c))
                        w.then_inc(vn_made, 1)
                        if c >= 1:
                            squares(f, pf, c - 1)
                    elif kind == "norm" and recur:
                        squares(f, pf, NC - 1)
                        act.wait_ge(squared, 2 * NC * (f + 1))
                        act.activation(ssq[:, :], ssq[:, :], ACT.Sqrt, scale=1.0 / DV,
                                       bias=mem.eps[:, 0:1]).then_inc(o_rms, 1)
                    elif entry == ("turn_o", 0) and finish:
                        for o in range(2):
                            split_hi(act, e, o, last, LAST * e + 1)
                    elif kind == "split_o" and finish:
                        for hh in range(2):
                            act.wait_ge(taken, LAST * e + 2 * hh + 2 + 2)
                            act.activation(mem.ah[:, hh, :], z[:, hh, :], ACT.Copy).then_inc(a_hi, 1)

            steps(act, step)

        @block.vector
        def _(dve):
            def step(h, p, solve, recur, finish):
                f, pf, e = h - 1, 1 - p, h - 2
                if recur:
                    wait(dve, rec, 4 * NC * f)
                    dve.memset(S[:, :], 0.0).then_inc(s_made, 1)
                for entry in ORDER:
                    kind = entry[0]
                    if kind == "decay" and solve:
                        g = entry[1]
                        filled(dve, h, entry)
                        if g >= 2:
                            vector_done(dve, h, ("products", g - 2))
                        elif not (isinstance(h, int) and h == 0):
                            vector_done(dve, h - 1, ("products", g + 2))
                        dve.tensor_tensor(Dg[:, g % 2, :, :], quad(solve_bank(entry)),
                                          mem.neg[:, :].unsqueeze(1).to_broadcast([P, 4, P]),
                                          ALU.add).then_inc(ev_v, 1)
                    elif kind == "products" and solve:
                        g = entry[1]
                        filled(dve, h, entry)
                        dve.wait_ge(decayed, GROUPS * h + g + 1)
                        ps = solve_bank(entry)
                        for x in range(4):
                            c, hh = 2 * g + x // 2, x % 2
                            dve.scalar_tensor_tensor(out=LN[:, 4 * g + x, :],
                                                     in0=ps[:, (x // 2) * 256:(x // 2) * 256 + P],
                                                     scalar=gate(p, "beta", hh, c), in1=Dg[:, g % 2, x, :],
                                                     op0=ALU.mult, op1=ALU.mult)
                        for cc in range(2):
                            w = dve.tensor_tensor(attn[:, p, 4 * g + 2 * cc:4 * g + 2 * cc + 2, :],
                                                  ps[:, cc * 256 + P:cc * 256 + 2 * P].unsqueeze(1)
                                                  .to_broadcast([P, 2, P]),
                                                  Dg[:, g % 2, 2 * cc:2 * cc + 2, :], ALU.mult)
                        w.then_inc(ev_v, 1)
                    elif kind == "left" and solve:
                        _, g, level = entry
                        filled(dve, h, entry)
                        if level == TOP:
                            dve.tensor_copy(LN[0:H, 4 * g:4 * g + 4, H:C], quarter(entry)).then_inc(ev_v, 1)
                            continue
                        dve.tensor_tensor(group(LN, g), quad(solve_bank(entry)),
                                          mem.mask[level][:, :].unsqueeze(1).to_broadcast([P, 4, P]),
                                          ALU.mult).then_inc(ev_v, 1)
                    elif kind == "right" and solve:
                        _, g, level = entry
                        filled(dve, h, entry)
                        if level == TOP:
                            dve.tensor_scalar(TT[0:H, p, 4 * g:4 * g + 4, H:C], quarter(entry), -1.0, None,
                                              ALU.mult).then_inc(ev_v, 1)
                            continue
                        dst = TT[:, p, 4 * g:4 * g + 4, :]
                        dve.scalar_tensor_tensor(out=dst.rearrange("p u n -> p (u n)"), in0=solve_bank(entry),
                                                 scalar=-1.0, in1=dst.rearrange("p u n -> p (u n)"),
                                                 op0=ALU.mult, op1=ALU.add).then_inc(ev_v, 1)
                    elif kind == "state" and recur:
                        c = entry[1]
                        dve.wait_ge(rec, 4 * (NC * f + c) + 1)
                        if c == 0:
                            parity_loaded(dve, v_in[pf], f, pf, 16)
                        for hh in range(2):
                            w = dve.scalar_tensor_tensor(out=r[:, hh * DV:(hh + 1) * DV],
                                                         in0=mem.ps[:, 3, hh * DV:(hh + 1) * DV],
                                                         scalar=gate(pf, "neg_eg", hh, c),
                                                         in1=v[:, pf, hh, c * DV:(c + 1) * DV],
                                                         op0=ALU.mult, op1=ALU.add)
                        w.then_inc(r_made, 1)
                    elif kind == "update" and recur:
                        c = entry[1]
                        dve.wait_ge(rec, 4 * (NC * f + c) + 4)
                        dve.wait_ge(s_made, (NC + 1) * f + c + 1)
                        for hh in range(2):
                            cols = slice(hh * DV, (hh + 1) * DV)
                            w = dve.scalar_tensor_tensor(out=S[:, cols], in0=S[:, cols],
                                                         scalar=gate(pf, "egl", hh, c), in1=mem.ps[:, 5, cols],
                                                         op0=ALU.mult, op1=ALU.add)
                        w.then_inc(s_made, 1)
                        dve.wait_ge(qs_made, NC * f + c + 1)
                        dve.wait_ge(r_made, NC * f + c + 1)
                        dve.tensor_tensor(v[:, pf, :, c * DV:(c + 1) * DV],
                                          mem.ps[:, 5, 2 * DV:4 * DV].rearrange("p (h d) -> p h d", h=2),
                                          qs[:, :].rearrange("p (h d) -> p h d", h=2), ALU.add).then_inc(o_made, 1)
                    elif kind == "norm" and recur:
                        dve.wait_ge(o_rms, f + 1)
                        dve.reciprocal(ssq[:, :], ssq[:, :]).then_inc(o_inv, 1)
                        dve.wait_ge(o_inv, f + 1)
                        for hh in range(2):
                            o = v[:, pf, hh, :].rearrange("p (c d) -> p c d", c=NC)
                            dve.tensor_tensor(o, o, ssq[:, hh * NC:(hh + 1) * NC].unsqueeze(2)
                                              .to_broadcast([P, NC, DV]), ALU.mult).then_inc(o_normed, 1)
                    elif kind == "turn_o" and finish:
                        n = entry[1]
                        dve.wait_ge(last, LAST * e + n + 1)
                        dve.wait_ge(z_in, 16 * e + 16)
                        dst = z[:, n // 2, (n % 2) * HALF:(n % 2 + 1) * HALF]
                        dve.scalar_tensor_tensor(out=dst, in0=bank(6 + n % 2), scalar=mem.par[:, 64:65], in1=dst,
                                                 op0=ALU.mult, op1=ALU.mult).then_inc(taken, 1)
                    elif kind == "out" and finish:
                        t = entry[1]
                        dve.wait_ge(last, LAST * e + 4 + t + 1)
                        dst = mem.x[:, t // 2, (t % 2) * HALF:(t % 2 + 1) * HALF]
                        dve.tensor_tensor(dst, bank(6 + t % 2), dst, ALU.add).then_inc(taken, 1)

            for b in range(2):
                dve.memset(S[:, b * DV:(b + 1) * DV], 0.0).then_inc(taken, 1)
            steps(dve, step)

        @block.tensor
        def _(pe):
            def step(h, p, solve, recur, finish):
                f, pf, e = h - 1, 1 - p, h - 2
                for entry in ORDER:
                    kind = entry[0]
                    if kind == "decay" and solve:
                        g = entry[1]
                        bank_free(pe, h, entry)
                        pe.wait_ge(gates_in, h + 1)
                        for x in range(4):
                            w = pe.matmul(solve_bank(entry)[:, x * P:(x + 1) * P],
                                          gate(p, "g", x % 2, 2 * g + x // 2).to_broadcast([P, P]),
                                          mem.upper[:, :], start=True, stop=True)
                        w.then_inc(fill, 1)
                    elif kind == "products" and solve:
                        g = entry[1]
                        bank_free(pe, h, entry)
                        if g == 0:
                            pe.wait_ge(solve_in, 32 * h + 32)
                        ps = solve_bank(entry)
                        for cc in range(2):
                            tokens = slice((2 * g + cc) * C, (2 * g + cc + 1) * C)
                            pe.matmul(ps[:, cc * 256:cc * 256 + P], kT[:, tokens], kT[:, tokens],
                                      start=True, stop=True)
                            w = pe.matmul(ps[:, cc * 256 + P:cc * 256 + 2 * P], kT[:, tokens],
                                          qT[:, tokens], start=True, stop=True)
                        w.then_inc(fill, 1)
                    elif kind == "turn_l" and solve:
                        g = entry[1]
                        bank_free(pe, h, entry)
                        vector_done(pe, h, ("products", g))
                        for x in range(4):
                            w = pe.transpose(solve_bank(entry)[:, x * P:(x + 1) * P], LN[:, 4 * g + x, :],
                                             mem.ident[:, :])
                        w.then_inc(fill, 1)
                    elif kind == "left" and solve:
                        _, g, level = entry
                        bank_free(pe, h, entry)
                        if level == LEVELS[0]:
                            scalar_done(pe, h, ("turn_l", g))
                            pe.wait_ge(inverses_in, 16 * NB * h + 16 * NB)
                        else:
                            vector_done(pe, h, ("right", g, level - 1))
                        if level == TOP:
                            for x in range(4):
                                w = pe.matmul(quarter(entry)[:, x, :], L[:, 4 * g + x, 0:H],
                                              TT[:, p, 4 * g + x, H:C], start=True, stop=True)
                            w.then_inc(fill, 1)
                            continue
                        for x in range(4):
                            w = pe.matmul(solve_bank(entry)[:, x * P:(x + 1) * P], L[:, 4 * g + x, :],
                                          unit(TT, p, 4 * g + x), start=True, stop=True)
                        w.then_inc(fill, 1)
                    elif kind == "turn_t" and solve:
                        _, g, level = entry
                        bank_free(pe, h, entry)
                        for x in range(4):
                            w = pe.transpose(solve_bank(entry)[:, x * P:(x + 1) * P], unit(TT, p, 4 * g + x),
                                             mem.ident[:, :])
                        w.then_inc(fill, 1)
                    elif kind == "right" and solve:
                        _, g, level = entry
                        bank_free(pe, h, entry)
                        vector_done(pe, h, ("left", g, level))
                        scalar_done(pe, h, ("turn_t", g, level))
                        if level == TOP:
                            for x in range(4):
                                w = pe.matmul(quarter(entry)[:, x, :], T[:, 4 * g + x, 0:H],
                                              LN[:, 4 * g + x, H:C], start=True, stop=True)
                            w.then_inc(fill, 1)
                            continue
                        for x in range(4):
                            w = pe.matmul(solve_bank(entry)[:, x * P:(x + 1) * P], T[:, 4 * g + x, :],
                                          LN[:, 4 * g + x, :], start=True, stop=True)
                        w.then_inc(fill, 1)
                    elif kind == "state" and recur:
                        c = entry[1]
                        tokens = slice(c * C, (c + 1) * C)
                        if c % 4 == 0:
                            pe.wait_ge(rec_in[c // 4], 48 * f + 48)
                        pe.wait_ge(s_made, (NC + 1) * f + c + 1)
                        wait(pe, vn_made, NC * f + c)
                        pe.matmul(mem.ps[:, 3, 0:2 * DV], rkT[:, tokens], S[:, :], start=True,
                                  stop=True).then_inc(rec, 1)
                        wait(pe, qs_made, NC * f + c)
                        pe.matmul(mem.ps[:, 4, 0:2 * DV], rqT[:, tokens], S[:, :], start=True,
                                  stop=True).then_inc(rec, 1)
                    elif kind == "solved" and recur:
                        c = entry[1]
                        pe.wait_ge(r_made, NC * f + c + 1)
                        if c == 0:
                            vector_done(pe, f, ("right", GROUPS - 1, TOP))
                        for hh in range(2):
                            cols = slice(hh * DV, (hh + 1) * DV)
                            w = pe.matmul(mem.ps[:, 3, cols], unit(TT, pf, 2 * c + hh), r[:, cols],
                                          start=True, stop=True)
                        w.then_inc(rec, 1)
                    elif kind == "update" and recur:
                        c = entry[1]
                        pe.wait_ge(vn_made, NC * f + c + 1)
                        wait(pe, o_made, NC * f + c)
                        pe.matmul(mem.ps[:, 5, 0:2 * DV], rk[:, c * DK:(c + 1) * DK], vd[:, :],
                                  start=True, stop=True)
                        for hh in range(2):
                            w = pe.matmul(mem.ps[:, 5, (2 + hh) * DV:(3 + hh) * DV], unit(attn, pf, 2 * c + hh),
                                          vn[:, hh * DV:(hh + 1) * DV], start=True, stop=True)
                        w.then_inc(rec, 1)
                    elif kind == "turn_o" and finish:
                        n = entry[1]
                        pe.wait_ge(o_normed, 2 * e + n // 2 + 1)
                        pe.wait_ge(taken, LAST * e + n + 1)
                        for q in range(4):
                            c = 4 * (n % 2) + q
                            w = pe.transpose(bank(6 + n % 2)[:, q * P:(q + 1) * P],
                                             v[:, p, n // 2, c * DV:(c + 1) * DV], mem.ident[:, :])
                        w.then_inc(last, 1)
                    elif kind == "out" and finish:
                        t = entry[1]
                        if t == 0:
                            pe.wait_ge(a_lo, 2 * e + 2)
                        if t % 8 == 0:
                            ready(pe, e, t // 8)
                        pe.wait_ge(taken, LAST * e + 4 + t + 1)
                        out_tile(pe, mem, t // 8, (t // 2) % 4, t % 2, 6 + t % 2).then_inc(last, 1)

            steps(pe, step)


def phase_finish(nc, sems, mem, io):
    with ExitStack() as ctx:
        rows = ctx.enter_context(nc.sbuf_tensor("fin_rows", [P, NC, D], F32))
        gain = ctx.enter_context(nc.sbuf_tensor("fin_gain", [P, D], F32))
        ssq = ctx.enter_context(nc.sbuf_tensor("fin_ssq", [P, NC, 2], F32))
        inv = ctx.enter_context(nc.sbuf_tensor("fin_inv", [P, NC], F32))
        gain_in = sems("fin_gain_in")
        turned = sems("fin_turned")
        squared = sems("fin_squared")
        summed = sems("fin_summed")
        root = sems("fin_root")
        inverse = sems("fin_inverse")
        kept = sems("fin_kept")
        stored = sems("fin_stored")
        block = ctx.enter_context(nc.Block())

        @block.sync
        def _(sp):
            sp.dma_start(gain[:, :], io.norm_final.partition_broadcast(P)).then_inc(gain_in, 16)
            for c in range(NC):
                sp.wait_ge(kept, 2 * c + 2)
                sp.dma_start(io.out[0, c * P:(c + 1) * P, :], rows[:, c, :]).then_inc(stored, 16)
            sp.wait_ge(stored, 16 * NC)

        @block.scalar
        def _(act):
            def rms(c):
                act.wait_ge(summed, c + 1)
                act.activation(inv[:, c:c + 1], inv[:, c:c + 1], ACT.Sqrt, scale=1.0 / D,
                               bias=mem.eps[:, 0:1]).then_inc(root, 1)

            for c in range(NC):
                for g in range(2):
                    act.wait_ge(turned, 2 * c + g + 1)
                    act.activation(rows[:, c, g * HALF:(g + 1) * HALF], mem.ps[:, (2 * c + g) % 8, :], ACT.Square,
                                   accum_out=ssq[:, c, g:g + 1]).then_inc(squared, 1)
                if c >= 1:
                    rms(c - 1)
            rms(NC - 1)

        @block.vector
        def _(dve):
            def sum_of(c):
                dve.wait_ge(squared, 2 * c + 2)
                dve.tensor_tensor(inv[:, c:c + 1], ssq[:, c, 0:1], ssq[:, c, 1:2], ALU.add).then_inc(summed, 1)

            sum_of(0)
            dve.wait_ge(gain_in, 16)
            for c in range(NC):
                if c < NC - 1:
                    sum_of(c + 1)
                dve.wait_ge(root, c + 1)
                dve.reciprocal(inv[:, c:c + 1], inv[:, c:c + 1]).then_inc(inverse, 1)
                dve.wait_ge(inverse, c + 1)
                for g in range(2):
                    dve.scalar_tensor_tensor(out=rows[:, c, g * HALF:(g + 1) * HALF], in0=mem.ps[:, (2 * c + g) % 8, :],
                                             scalar=inv[:, c:c + 1], in1=gain[:, g * HALF:(g + 1) * HALF],
                                             op0=ALU.mult, op1=ALU.mult).then_inc(kept, 1)

        @block.tensor
        def _(pe):
            for t in range(2 * NC):
                c, g = t // 2, t % 2
                wait(pe, kept, t - 7)
                for q in range(4):
                    last = pe.transpose(mem.ps[:, t % 8, q * P:(q + 1) * P],
                                        mem.x[:, 4 * g + q, c * P:(c + 1) * P], mem.ident[:, :])
                last.then_inc(turned, 1)


class Names:
    pass


def build(nc, io, phases=("sc", "ffn0", "gdn", "ffn1")):
    mem = Names()
    with ExitStack() as ctx:
        def sb(name, shape, dt=F32):
            return ctx.enter_context(nc.sbuf_tensor(name, shape, dt))

        def sems(name):
            return ctx.enter_context(nc.semaphore(name))

        mem.par_rows = {"par": 65, "ffn": 2 * FFN_TAPS * 2 * FT}
        mem.x = sb("x_res", [P, KT, SEQ])
        mem.raw = sb("w_raw", [P, 2, WCOLS])
        mem.wh = [sb(f"w_hi{s}", [P, WCOLS], F32R) for s in range(2)]
        mem.wl = [sb(f"w_lo{s}", [P, WCOLS], F32R) for s in range(2)]
        mem.ident, mem.ones, mem.eps = sb("ident", [P, P]), sb("ones", [P, P]), sb("eps", [P, 1])
        mem.par = sb("par", [P, mem.par_rows["par"]])
        mem.fcw = sb("ffn_taps", [P, mem.par_rows["ffn"]])
        mem.gcw = sb("gdn_taps", [P, P])
        mem.alog, mem.dtb = sb("a_log", [P, NV]), sb("dt_bias", [P, NV])
        mem.ps = ctx.enter_context(nc.psum_tensor("ps", [P, 8, HALF], F32))
        mem.first_in, mem.first_count = sems("first_in"), 0
        mem.first_jobs = [first_weights(io, phase) for phase in phases]
        phase_load(nc, sems, mem, io)
        if "sc" in phases:
            phase_mix(nc, sems, mem, io, "sc", 0)
        if "ffn0" in phases:
            phase_mix(nc, sems, mem, io, "ffn", 0)
        if "gdn" in phases:
            phase_gdn(nc, sems, mem, io)
        if "ffn1" in phases:
            phase_mix(nc, sems, mem, io, "ffn", 1)
        phase_finish(nc, sems, mem, io)


INPUTS = ["x", "norm_mix", "norm_ffn", "sc_w_in", "sc_conv", "sc_w_out", "gdn_w_in", "gdn_conv", "gdn_a_log",
          "gdn_dt_bias", "gdn_norm", "gdn_w_out", "ffn_w_up", "ffn_conv", "ffn_w_down", "norm_final"]


def kernel(**inputs):
    import numpy as np
    import concourse.bacc as bacc
    from concourse.bass_utils import run_bass_kernel_spmd

    nc = bacc.Bacc("TRN2", target_bir_lowering=False, num_devices=1)
    io, arrays = Names(), {}
    for name in INPUTS:
        a = np.ascontiguousarray(inputs[name])
        arrays[f"in_{name}"] = a
        io.__dict__[name] = nc.dram_tensor(f"in_{name}", a.shape, F32, kind="ExternalInput").ap()
    io.out = nc.dram_tensor("out", [1, SEQ, D], F32, kind="ExternalOutput").ap()
    build(nc, io)
    result = run_bass_kernel_spmd(nc, [arrays], core_ids=[0])
    return result.results[0]["out"]
```
